# Optimizing a Trainium2 kernel written in Bass

```python
import math
import jax, jax.numpy as jnp
from jax import lax
import numpy as np

D_MODEL = 1024
BATCH = 1
SEQ = 256
DEPTH = 2

ROPE_THETA = 500000.0
NORM_EPS = 1e-6
LN_EPS = 1e-5
Q_BLOCK = 128
N_EVEN = (DEPTH + 1) // 2
N_ODD = DEPTH // 2

A_WIDTH = D_MODEL // 2
A_QK_DIM = 64
A_HEADS = A_WIDTH // (2 * A_QK_DIM)
A_V_DIM = 2 * A_QK_DIM
A_ROT = A_QK_DIM // 4

B_WIDTH = D_MODEL // 2
B_GROUPS = 4
B_GROUP_CH = B_WIDTH // B_GROUPS
B_CHUNK = 128

EVEN_IN = 3 * A_WIDTH + 2 * B_WIDTH

C_WIDTH = D_MODEL // 2
C_WINDOWS = (2, 4, 8, 16)
C_GROUPS = len(C_WINDOWS)
C_GROUP_CH = C_WIDTH // C_GROUPS

D_HEADS = 8
D_NOPE = 64
D_ROPE = 32
D_V = 64
D_Q_RANK = 384
D_KV_RANK = 256
D_WIDTH = D_HEADS * D_V

ODD_IN = C_WIDTH + D_Q_RANK + D_KV_RANK + D_ROPE

FFN_DENSE = 2816
N_EXPERTS = 8
TOP_K = 2
FFN_EXPERT = 3584

kernel_name = "hybrid_diffattn_sgu_pool_mla_moe"

def _rmsnorm(x, g):
    xf = x.astype(jnp.float32)
    y = xf * lax.rsqrt(jnp.mean(xf * xf, axis=-1, keepdims=True) + NORM_EPS)
    return (y * g.astype(jnp.float32)).astype(x.dtype)

def _layernorm(x, g, b):
    xf = x.astype(jnp.float32)
    mu = jnp.mean(xf, axis=-1, keepdims=True)
    var = jnp.mean(jnp.square(xf - mu), axis=-1, keepdims=True)
    y = (xf - mu) * lax.rsqrt(var + LN_EPS)
    return (y * g.astype(jnp.float32) + b.astype(jnp.float32)).astype(x.dtype)

def _rope_tables(seq, rot_dim):
    pos = jnp.arange(seq, dtype=jnp.float32)
    inv = ROPE_THETA ** (-jnp.arange(0, rot_dim, 2, dtype=jnp.float32) / rot_dim)
    ang = pos[:, None] * inv[None, :]
    return jnp.cos(ang), jnp.sin(ang)

def _apply_rope(x, cos, sin, rot_dim):
    half = rot_dim // 2
    shape = (x.shape[1],) + (1,) * (x.ndim - 3) + (half,)
    c = cos.reshape(shape)
    s = sin.reshape(shape)
    xf = x.astype(jnp.float32)
    x1 = xf[..., :half]
    x2 = xf[..., half:rot_dim]
    out = jnp.concatenate([x1 * c - x2 * s, x2 * c + x1 * s, xf[..., rot_dim:]], axis=-1)
    return out.astype(x.dtype)

def _to_blocks(t):
    b, h, s, d = t.shape
    return t.reshape(b, h, s // Q_BLOCK, Q_BLOCK, d).transpose(2, 0, 1, 3, 4)

def _from_blocks(o):
    nb, b, h, qb, d = o.shape
    return o.transpose(1, 0, 3, 2, 4).reshape(b, nb * qb, h, d)

def _block_causal_probs(q_blk, k, q_start, scale):
    s = jnp.einsum('bhqd,bhkd->bhqk', q_blk, k).astype(jnp.float32) * scale
    q_pos = q_start + jnp.arange(q_blk.shape[2])
    k_pos = jnp.arange(k.shape[2])
    s = jnp.where(k_pos[None, :] <= q_pos[:, None], s, -jnp.inf)
    return jax.nn.softmax(s, axis=-1)

def _diff_attention(q, k, v, lam, scale):
    nb = q.shape[3] // Q_BLOCK
    starts = jnp.arange(nb) * Q_BLOCK
    k1 = k[:, :, 0]
    k2 = k[:, :, 1]

    def blk(args):
        q1b, q2b, st = args
        p = _block_causal_probs(q1b, k1, st, scale) - lam * _block_causal_probs(q2b, k2, st, scale)
        return jnp.einsum('bhqk,bhkd->bhqd', p.astype(v.dtype), v)

    return _from_blocks(lax.map(blk, (_to_blocks(q[:, :, 0]), _to_blocks(q[:, :, 1]), starts)))

def _causal_attention(q, k, v, scale):
    nb = q.shape[2] // Q_BLOCK
    starts = jnp.arange(nb) * Q_BLOCK

    def blk(args):
        qb, st = args
        p = _block_causal_probs(qb, k, st, scale)
        return jnp.einsum('bhqk,bhkd->bhqd', p.astype(v.dtype), v)

    return _from_blocks(lax.map(blk, (_to_blocks(q), starts)))

def _even_mixer(h, layer_idx, w_in, lam_q1, lam_k1, lam_q2, lam_k2, subln_g,
                sgu_ln_g, sgu_ln_b, sgu_w, sgu_b, w_out, cos_a, sin_a):
    b, s, _ = h.shape
    proj = h @ w_in
    qa, ka, va, ub, vb = jnp.split(
        proj, [A_WIDTH, 2 * A_WIDTH, 3 * A_WIDTH, 3 * A_WIDTH + B_WIDTH], axis=-1)

    qa = _apply_rope(qa.reshape(b, s, A_HEADS, 2, A_QK_DIM), cos_a, sin_a, A_ROT).transpose(0, 2, 3, 1, 4)
    ka = _apply_rope(ka.reshape(b, s, A_HEADS, 2, A_QK_DIM), cos_a, sin_a, A_ROT).transpose(0, 2, 3, 1, 4)
    va = va.reshape(b, s, A_HEADS, A_V_DIM).transpose(0, 2, 1, 3)
    lam_init = 0.8 - 0.6 * math.exp(-0.3 * layer_idx)
    f32 = jnp.float32
    lam = (jnp.exp(jnp.sum(lam_q1.astype(f32) * lam_k1.astype(f32)))
           - jnp.exp(jnp.sum(lam_q2.astype(f32) * lam_k2.astype(f32))) + lam_init)
    oa = _diff_attention(qa, ka, va, lam, A_QK_DIM ** -0.5)
    oa = (_rmsnorm(oa, subln_g) * (1.0 - lam_init)).reshape(b, s, A_WIDTH)

    ub = jax.nn.gelu(ub)
    vb = _layernorm(jax.nn.gelu(vb), sgu_ln_g, sgu_ln_b)
    n = s // B_CHUNK
    vb = vb.reshape(b, n, B_CHUNK, B_GROUPS, B_GROUP_CH)
    causal = jnp.tril(jnp.ones((B_CHUNK, B_CHUNK), dtype=bool))
    ws = jnp.where(causal[None], sgu_w, 0)
    mixed = jnp.einsum('gpq,bnqgc->bnpgc', ws, vb) + sgu_b.T[None, None, :, :, None]
    ob = (ub.reshape(b, n, B_CHUNK, B_GROUPS, B_GROUP_CH) * mixed).reshape(b, s, B_WIDTH)

    return jnp.concatenate([oa, ob], axis=-1) @ w_out

def _odd_mixer(h, w_in, pool_w, pool_scale, q_norm_g, w_uq, kv_norm_g, w_ukv, w_out, cos_d, sin_d):
    b, s, _ = h.shape
    proj = h @ w_in
    xc, cq, ckv, kpe = jnp.split(
        proj, [C_WIDTH, C_WIDTH + D_Q_RANK, C_WIDTH + D_Q_RANK + D_KV_RANK], axis=-1)

    csum = jnp.pad(jnp.cumsum(xc.astype(jnp.float32), axis=1), ((0, 0), (1, 0), (0, 0)))
    pos = jnp.arange(s)
    groups = []
    for g, w in enumerate(C_WINDOWS):
        sl = slice(g * C_GROUP_CH, (g + 1) * C_GROUP_CH)
        lo = jnp.maximum(pos + 1 - w, 0)
        win_sum = csum[:, 1:, sl] - csum[:, lo, sl]
        cnt = jnp.minimum(pos + 1, w).astype(jnp.float32)[None, :, None]
        groups.append(win_sum / cnt - xc[..., sl].astype(jnp.float32))
    pooled = jnp.stack(groups, axis=2).astype(h.dtype)
    oc = jnp.einsum('bsgc,gcd->bsgd', pooled, pool_w).reshape(b, s, C_WIDTH) * pool_scale

    q = (_rmsnorm(cq, q_norm_g) @ w_uq).reshape(b, s, D_HEADS, D_NOPE + D_ROPE)
    q = jnp.concatenate([q[..., :D_NOPE], _apply_rope(q[..., D_NOPE:], cos_d, sin_d, D_ROPE)], axis=-1)
    kv = (_rmsnorm(ckv, kv_norm_g) @ w_ukv).reshape(b, s, D_HEADS, D_NOPE + D_V)
    kpe = _apply_rope(kpe[:, :, None, :], cos_d, sin_d, D_ROPE)
    k = jnp.concatenate([kv[..., :D_NOPE], jnp.broadcast_to(kpe, (b, s, D_HEADS, D_ROPE))], axis=-1)
    v = kv[..., D_NOPE:]
    od = _causal_attention(q.transpose(0, 2, 1, 3), k.transpose(0, 2, 1, 3), v.transpose(0, 2, 1, 3),
                           (D_NOPE + D_ROPE) ** -0.5).reshape(b, s, D_WIDTH)

    return jnp.concatenate([oc, od], axis=-1) @ w_out

def _swiglu(x, wg, wu, wd):
    return (jax.nn.silu(x @ wg) * (x @ wu)) @ wd

def _moe(x, router, wg, wu, wd):
    logits = (x @ router).astype(jnp.float32)
    top_val, top_idx = lax.top_k(logits, TOP_K)
    top_w = jax.nn.softmax(top_val, axis=-1)
    gate = jnp.sum(jax.nn.one_hot(top_idx, N_EXPERTS, dtype=jnp.float32) * top_w[..., None], axis=-2)
    y = jnp.zeros_like(x)
    for e in range(N_EXPERTS):
        y = y + gate[..., e:e + 1].astype(x.dtype) * _swiglu(x, wg[e], wu[e], wd[e])
    return y

def setup_inputs(seed: int = 0) -> dict:
    key = jax.random.key(seed)
    ks = iter(jax.random.split(key, 40))
    f32 = jnp.float32

    def nrm(shape, scale):
        return jax.random.normal(next(ks), shape, f32) * scale

    def gain(shape):
        return 1.0 + 0.02 * jax.random.normal(next(ks), shape, f32)

    D = D_MODEL
    return {
        "x": nrm((BATCH, SEQ, D), 1.0),
        "norm_mix_even": gain((N_EVEN, D)),
        "w_in_even": nrm((N_EVEN, D, EVEN_IN), D ** -0.5),
        "lam_q1": nrm((N_EVEN, A_QK_DIM), 0.1),
        "lam_k1": nrm((N_EVEN, A_QK_DIM), 0.1),
        "lam_q2": nrm((N_EVEN, A_QK_DIM), 0.1),
        "lam_k2": nrm((N_EVEN, A_QK_DIM), 0.1),
        "subln_g": gain((N_EVEN, A_V_DIM)),
        "sgu_ln_g": gain((N_EVEN, B_WIDTH)),
        "sgu_ln_b": nrm((N_EVEN, B_WIDTH), 0.02),
        "sgu_w": nrm((N_EVEN, B_GROUPS, B_CHUNK, B_CHUNK), B_CHUNK ** -0.5),
        "sgu_b": gain((N_EVEN, B_GROUPS, B_CHUNK)),
        "w_out_even": nrm((N_EVEN, A_WIDTH + B_WIDTH, D), (A_WIDTH + B_WIDTH) ** -0.5),
        "norm_ffn_even": gain((N_EVEN, D)),
        "ffn_wg": nrm((N_EVEN, D, FFN_DENSE), D ** -0.5),
        "ffn_wu": nrm((N_EVEN, D, FFN_DENSE), D ** -0.5),
        "ffn_wd": nrm((N_EVEN, FFN_DENSE, D), FFN_DENSE ** -0.5),
        "norm_mix_odd": gain((N_ODD, D)),
        "w_in_odd": nrm((N_ODD, D, ODD_IN), D ** -0.5),
        "pool_w": nrm((N_ODD, C_GROUPS, C_GROUP_CH, C_GROUP_CH), C_GROUP_CH ** -0.5),
        "pool_scale": 1.0 + 0.1 * jax.random.normal(next(ks), (N_ODD, C_WIDTH), f32),
        "q_norm_g": gain((N_ODD, D_Q_RANK)),
        "w_uq": nrm((N_ODD, D_Q_RANK, D_HEADS * (D_NOPE + D_ROPE)), D_Q_RANK ** -0.5),
        "kv_norm_g": gain((N_ODD, D_KV_RANK)),
        "w_ukv": nrm((N_ODD, D_KV_RANK, D_HEADS * (D_NOPE + D_V)), D_KV_RANK ** -0.5),
        "w_out_odd": nrm((N_ODD, C_WIDTH + D_WIDTH, D), (C_WIDTH + D_WIDTH) ** -0.5),
        "norm_ffn_odd": gain((N_ODD, D)),
        "router": nrm((N_ODD, D, N_EXPERTS), D ** -0.5),
        "moe_wg": nrm((N_ODD, N_EXPERTS, D, FFN_EXPERT), D ** -0.5),
        "moe_wu": nrm((N_ODD, N_EXPERTS, D, FFN_EXPERT), D ** -0.5),
        "moe_wd": nrm((N_ODD, N_EXPERTS, FFN_EXPERT, D), FFN_EXPERT ** -0.5),
        "final_norm": gain((D,)),
    }

def reference(x, norm_mix_even, w_in_even, lam_q1, lam_k1, lam_q2, lam_k2, subln_g,
              sgu_ln_g, sgu_ln_b, sgu_w, sgu_b, w_out_even, norm_ffn_even, ffn_wg, ffn_wu, ffn_wd,
              norm_mix_odd, w_in_odd, pool_w, pool_scale, q_norm_g, w_uq, kv_norm_g, w_ukv,
              w_out_odd, norm_ffn_odd, router, moe_wg, moe_wu, moe_wd, final_norm):
    s = x.shape[1]
    cos_a, sin_a = _rope_tables(s, A_ROT)
    cos_d, sin_d = _rope_tables(s, D_ROPE)
    h = x
    for l in range(DEPTH):
        i = l // 2
        if l % 2 == 0:
            h = h + _even_mixer(_rmsnorm(h, norm_mix_even[i]), l, w_in_even[i],
                                lam_q1[i], lam_k1[i], lam_q2[i], lam_k2[i], subln_g[i],
                                sgu_ln_g[i], sgu_ln_b[i], sgu_w[i], sgu_b[i], w_out_even[i],
                                cos_a, sin_a)
            h = h + _swiglu(_rmsnorm(h, norm_ffn_even[i]), ffn_wg[i], ffn_wu[i], ffn_wd[i])
        else:
            h = h + _odd_mixer(_rmsnorm(h, norm_mix_odd[i]), w_in_odd[i], pool_w[i], pool_scale[i],
                               q_norm_g[i], w_uq[i], kv_norm_g[i], w_ukv[i], w_out_odd[i],
                               cos_d, sin_d)
            h = h + _moe(_rmsnorm(h, norm_ffn_odd[i]), router[i], moe_wg[i], moe_wu[i], moe_wd[i])
    return _rmsnorm(h, final_norm)


_drawn_inputs = setup_inputs


def setup_inputs(seed=0):
    import zlib

    import numpy as np

    out = dict(_drawn_inputs(seed))
    spreads = {}
    factors = {'lam_q2': 60.289,
     'sgu_ln_g': 3.633,
     'sgu_ln_b': 4.08,
     'sgu_b': 3.348,
     'norm_mix_odd': 2.831,
     'q_norm_g': 8.0,
     'kv_norm_g': 3.982,
     'final_norm': 8.392,
     'norm_ffn_odd': 7.332}
    for name, (base, spread) in spreads.items():
        noise = np.random.default_rng([zlib.crc32(name.encode()), seed]).standard_normal(out[name].shape)
        drawn = base * np.exp(spread * noise) if base else spread * noise
        out[name] = __import__('jax').numpy.asarray(drawn.astype(out[name].dtype))
    for name, factor in factors.items():
        out[name] = (out[name] * factor).astype(out[name].dtype)
    return out
```

```python
import math
from contextlib import ExitStack

import numpy as np

import concourse.bass as bass
from concourse import mybir

F32 = mybir.dt.float32
F32R = mybir.dt.float32r
I32 = mybir.dt.int32
ALU = mybir.AluOpType
ACT = mybir.ActivationFunctionType
AX = mybir.AxisListType

P = 128
D = 1024
S = 256
T = S // P
KC = D // P
NORM_EPS = 1e-6
LN_EPS = 1e-5
MAPS = 8
A_HEADS, A_QK, A_HALF = 4, 64, 8
D_QK, D_NOPE, D_HALF, D_V = 96, 64, 16, 64
A_SCALE = A_QK ** -0.5
D_SCALE = D_QK ** -0.5
LAM_INIT = 0.8 - 0.6 * math.exp(0.0)
FFN = 2816
NE, FE = 8, 3584
FB = FE // 512
SLOTS = P
EXTRA = 2 * S // (SLOTS + 1)
ITEMS = NE + EXTRA
NEG = -1e30
CQ, CKV = 384, 256
WINDOWS = (2, 4, 8, 16)

CONST = {}
_at = 0
for _n, _w in (("ident", P), ("causal", P), ("iota", P), ("before", P), ("ones", P), ("ropeA", 2 * T * A_HALF),
               ("ropeD", 2 * T * D_HALF), ("lower8", NE * NE), ("iota8", NE)):
    CONST[_n] = (_at, _at + _w)
    _at += _w
CONSTS = _at


def constants():
    def rope(rot):
        f = np.float32
        inv = f(500000.0) ** (-np.arange(0, rot, 2, dtype=f) / f(rot))
        ang = np.arange(S, dtype=f)[:, None] * inv[None, :].astype(f)
        both = np.stack([np.cos(ang), np.sin(ang)])
        return both.reshape(2, T, P, rot // 2).transpose(2, 0, 1, 3).reshape(P, -1)
    i = np.arange(P)
    lower8 = (np.arange(NE)[None, :] < np.arange(NE)[:, None]).astype(np.float32).reshape(-1)
    parts = dict(ident=np.eye(P), causal=np.where(i[None, :] <= i[:, None], 0.0, NEG),
                 iota=np.tile(i, (P, 1)), before=(i[:, None] < i[None, :]), ones=np.ones((P, P)),
                 ropeA=rope(2 * A_HALF), ropeD=rope(2 * D_HALF),
                 lower8=np.tile(lower8, (P, 1)), iota8=np.tile(np.arange(NE), (P, 1)))
    table = np.concatenate([np.asarray(parts[n], np.float32) for n in CONST], axis=1)
    band = np.zeros((S, len(WINDOWS), S), np.float32)
    for g, w in enumerate(WINDOWS):
        for t in range(S):
            lo = max(t + 1 - w, 0)
            band[lo:t + 1, g, t] = np.float32(1.0) / np.float32(min(t + 1, w))
            band[t, g, t] -= 1.0
    bands = np.concatenate([band[:P], band[P:, :, P:]], axis=2)
    return table, np.ascontiguousarray(bands)


class Unit:
    def __init__(self, src, shape, quantum, first):
        self.src, self.shape, self.quantum = src, shape, quantum
        self.size = int(np.prod(shape))
        self.quanta = self.size // quantum
        self.first = first


def columns(w, c0, c1):
    return w[:, c0:c1].rearrange("(c p) n -> p c n", p=P)


def trunk(nc, A, consts_d, bands_d, out):
    units, groups = [], {}

    def add(name, src, shape, quantum):
        u = Unit(src, shape, quantum, units[-1].first + units[-1].quanta if units else 0)
        groups.setdefault(name, []).append(len(units))
        units.append(u)

    w_in_e, w_out_e = A["w_in_even"][0], A["w_out_even"][0]
    for b in range(5):
        add("in_even", columns(w_in_e, 512 * b, 512 * b + 512), (KC, 512), 1024)
    for b in range(2):
        add("out_even", columns(w_out_e, 512 * b, 512 * b + 512), (KC, 512), 1024)
    widths = [min(512, FFN - f) for f in range(0, FFN, 512)]

    def add_down(f):
        w = widths[f]
        add("down", A["ffn_wd"][0][512 * f:512 * f + w, :].rearrange("(c p) n -> p c n", p=P), (w // P, D), 1024)

    for f, w in enumerate(widths):
        for name in ("wg", "wu"):
            add("gate" if name == "wg" else "up", columns(A["ffn_" + name][0], 512 * f, 512 * f + w), (KC, w), 1024)
        if f:
            add_down(f - 1)
    add_down(len(widths) - 1)
    w_in_o = A["w_in_odd"][0]
    for c0, c1 in ((0, 512), (512, 512 + CQ), (512 + CQ, 1184)):
        add("in_odd", columns(w_in_o, c0, c1), (KC, c1 - c0), 2 * (c1 - c0))
    add("uq", A["w_uq"][0].rearrange("(c p) n -> p c n", p=P), (3, 768), 768)
    add("ukv", A["w_ukv"][0].rearrange("(c p) n -> p c n", p=P), (2, 1024), 1024)
    for b in range(2):
        add("out_odd", columns(A["w_out_odd"][0], 512 * b, 512 * b + 512), (KC, 512), 1024)
    U1 = len(units)
    Q1 = units[-1].first + units[-1].quanta
    quanta = [(u, k) for u, unit in enumerate(units) for k in range(unit.quanta)]
    RING1, RING2, NQ = 4, 7, 4
    ORDER = []
    for f in range(FB):
        ORDER += [("gate", f), ("up", f)]
        if f:
            ORDER.append(("down", f - 1))
    ORDER.append(("down", FB - 1))
    UI = len(ORDER)
    QI = 4 * UI
    assert UI % RING2 == 0 and QI % NQ == 0 and U1 % RING1 == 0
    pos_of = {o: n for n, o in enumerate(ORDER)}

    fills, n = {}, 0
    for name, k in (("mix_even", 4), ("qk_a", 8), ("sgu_w", 1), ("mixed", 2), ("pT_a", 6), ("cat_even", 4), ("ffn", 4),
                    ("mix_odd", 4), ("pooled", 4), ("poolout", 4), ("cq", 2), ("ckv", 1), ("qk_d", 8), ("pT_d", 6),
                    ("cat_odd", 2), ("router", 4), ("logits", 1), ("prefix", 1)):
        fills[name] = n
        n += k

    fills["pT_a1"], fills["pT_d1"] = fills["pT_a"] + 2, fills["pT_d"] + 2

    with ExitStack() as ctx:
        def sbuf(name, shape, dt=F32, on=ctx):
            return on.enter_context(nc.sbuf_tensor(name, [P] + list(shape), dt))

        def sem(name):
            return ctx.enter_context(nc.semaphore(name))

        ring_a = sbuf("ring_a", [RING1, 4096])
        w_hi = sbuf("w_hi", [NQ, 1024], F32R)
        w_lo = sbuf("w_lo", [NQ, 1024], F32R)
        h = sbuf("h", [T, D])
        table = sbuf("table", [CONSTS])
        stats = sbuf("stats", [72])
        slot_of = sbuf("slot_of", [T, ITEMS])
        gate_of = sbuf("gate_of", [T, ITEMS])
        active = ctx.enter_context(nc.sbuf_tensor("active", [1, ITEMS], I32))
        expert = ctx.enter_context(nc.sbuf_tensor("expert", [1, ITEMS], I32))
        xn = sbuf("xn", [T, D])
        xt_hi = sbuf("xt_hi", [KC, S], F32R)
        xt_lo = sbuf("xt_lo", [KC, S], F32R)
        gain = sbuf("gain", [D])

        even = ExitStack()
        proj = sbuf("proj", [T, 2560], on=even)
        qT = sbuf("qT", [MAPS, S], on=even)
        kT = sbuf("kT", [MAPS, S], on=even)
        e = sbuf("e", [MAPS, S], on=even)
        eT = sbuf("eT", [T, MAPS, P], on=even)
        sgu_w = sbuf("sgu_w_sb", [4, P], on=even)
        sgu_wT = sbuf("sgu_wT", [4, P], on=even)
        sgu_b = sbuf("sgu_b_sb", [4], on=even)
        subln = sbuf("subln", [P], on=even)
        lamv = sbuf("lamv", [4, 64], on=even)
        lamj = sbuf("lamj", [2, 64], on=even)
        even.close()
        dense = ExitStack()
        f_hi = sbuf("f_hi", [2, 4, S], F32R, on=dense)
        f_lo = sbuf("f_lo", [2, 4, S], F32R, on=dense)
        dense.close()
        odd = ExitStack()
        proj2 = sbuf("proj2", [T, 1184], on=odd)
        qT2 = sbuf("qT2", [MAPS, S], on=odd)
        kT2 = sbuf("kT2", [MAPS, S], on=odd)
        e2 = sbuf("e2", [MAPS, S], on=odd)
        eT2 = sbuf("eT2", [T, MAPS, P], on=odd)
        qf = sbuf("qf", [T, MAPS, D_QK], on=odd)
        kv = sbuf("kv", [T, MAPS, 2 * D_NOPE], on=odd)
        pool_w = sbuf("pool_w_sb", [4, P], on=odd)
        pool_s = sbuf("pool_s", [4], on=odd)
        c_hi = sbuf("c_hi", [5, S], F32R, on=odd)
        c_lo = sbuf("c_lo", [5, S], F32R, on=odd)
        odd.close()
        route = ExitStack()
        xT = sbuf("xT", [KC, S], on=route)
        rw = sbuf("rw", [KC, NE], on=route)
        lg = sbuf("lg", [T, NE], on=route)
        top = sbuf("top", [T, 8], on=route)
        cmp1 = sbuf("cmp1", [T, NE, NE], on=route)
        cmp2 = sbuf("cmp2", [T, NE, NE], on=route)
        rank = sbuf("rank", [T, NE], on=route)
        sel = sbuf("sel", [T, NE], on=route)
        gate = sbuf("gate", [T, NE], on=route)
        gtmp = sbuf("gtmp", [T, NE], on=route)
        place = sbuf("place", [T, NE], on=route)
        over = sbuf("over", [4, NE], on=route)
        wts = sbuf("wts", [T, 4], on=route)
        route.close()
        xg_hi = sbuf("xg_hi", [KC, P], F32R)
        xg_lo = sbuf("xg_lo", [KC, P], F32R)
        hT_hi = sbuf("hT_hi", [4, P], F32R)
        hT_lo = sbuf("hT_lo", [4, P], F32R)
        y_hi = sbuf("y_hi", [D], F32R)
        y_lo = sbuf("y_lo", [D], F32R)
        pick = sbuf("pick", [T, SLOTS], F32R)
        pickT = sbuf("pickT", [S], F32R)
        ring_b = sbuf("ring_b", [RING2 - RING1, 4096])
        g_act = xn[:, 0, 0:512]
        g_mul = xn[:, 0, 512:1024]
        xn_hi = xt_hi[:, :, :].rearrange("p c s -> p (c s)").rearrange("p (t d) -> p t d", t=T)
        xn_lo = xt_lo[:, :, :].rearrange("p c s -> p (c s)").rearrange("p (t d) -> p t d", t=T)
        kf = xn[:, :, 0:768].rearrange("p t (m d) -> p t m d", m=MAPS)
        bands = eT2[:, :, :, :].rearrange("p t m q -> p (t m q)")[:, 0:4 * 384].rearrange("p (g s) -> p g s", g=4)
        pooledT = e2[:, 0:4, :]

        ps = ctx.enter_context(nc.psum_tensor("ps", [P, 8, 512], F32))
        flat = ps[:, :, :].rearrange("p b n -> p (b n)")

        def st(name, k=0, n=None):
            at, w = dict(SSQ=(0, 8), MS=(8, 8), ROOT=(16, 8), NEGMAX=(24, 8), ESUM=(32, 8), MAX=(40, 8), EINV=(48, 8),
                         SUM=(56, 2), NEGMU=(58, 2), VSQ=(60, 2), LDOT=(62, 2), LEXP=(64, 2), NLAM=(66, 1), TMP=(67, 1),
                         JUNK=(68, 1), MARK=(69, 1))[name]
            return stats[:, at + k:at + k + (w if n is None else n)]

        def con(name):
            a, b = CONST[name]
            return table[:, a:b]
        ident = con("ident")

        def slot(s):
            return ring_a[:, s] if s < RING1 else ring_b[:, s - RING1]

        const_in, x_in, gain_in, even_in, bands_in, odd_in, rw_in = map(sem, (
            "const_in", "x_in", "gain_in", "even_in", "bands_in", "odd_in", "rw_in"))
        loaded = [sem(f"loaded{s}") for s in range(RING2)]
        hi_done, lo_done, q_used = sem("hi_done"), sem("lo_done"), sem("q_used")
        t_ready = [sem("t_ready0"), sem("t_ready1")]
        t_free = [sem("t_free0"), sem("t_free1")]
        t_head = sem("t_head")
        blk_free = [sem("blk_free0"), sem("blk_free1")]
        ssq_done, ms_done, root_done, xn_done = map(sem, ("ssq_done", "ms_done", "root_done", "xn_done"))
        act_chain, dve_chain = sem("act_chain"), sem("dve_chain")
        roped, lam_dot, lam_exp = sem("roped"), sem("lam_dot"), sem("lam_exp")
        mu_done, vsq_done, ln_applied, oa_done = map(sem, ("mu_done", "vsq_done", "ln_applied", "oa_done"))
        sgu_masked = sem("sgu_masked")
        scored, negmax, exped, o_ready, o_free = map(sem, ("scored", "negmax", "exped", "o_ready", "o_free"))
        fsilu, fmul, f_head, f_done, down_added = map(sem, ("fsilu", "fmul", "f_head", "f_done", "down_added"))
        kf_done, big_free = sem("kf_done"), sem("big_free")
        h_done = sem("h_done")
        top_done, top_exp, sel_done, routed, xn_head, xn_rest = map(sem, ("top_done", "top_exp", "sel_done", "routed", "xn_head", "xn_rest"))
        picked, gathered, pickT_ready, pickT_done, xg_head, xg_rest = map(sem, (
            "picked", "gathered", "pickT_ready", "pickT_done", "xg_head", "xg_rest"))
        silu_done, mul_done, hT_ready, hT_head, hT_rest = map(sem, (
            "silu_done", "mul_done", "hT_ready", "hT_head", "hT_rest"))
        y_head, y_rest, scattered, added = map(sem, ("y_head", "y_rest", "scattered", "added"))
        experts_done, out_ready, stored = sem("experts_done"), sem("out_ready"), sem("stored")

        block = ctx.enter_context(nc.Block())

        def filled(k):
            return t_ready[k % 2], k // 2 + 1

        def emptied(k):
            return t_free[k % 2], k // 2 + 1

        blocks = [u for name in ("in_even", "out_even", "in_odd", "out_odd") for u in groups[name]]
        block_no = {u: n for n, u in enumerate(blocks)}

        taken, seen = [], [0, 0, 0]
        for n, u in enumerate(blocks):
            if u in groups["out_even"] + groups["out_odd"]:
                seen[2] += 1
                taken.append((h_done, seen[2]))
            else:
                seen[n % 2] += 1
                taken.append((blk_free[n % 2], seen[n % 2]))

        def used(u):
            return q_used, units[u].first + units[u].quanta

        def block_banks(n):
            return 2 * (n % 2)

        @block.sync
        def _(sp):
            sp.dma_start(h[:, :, :], A["x"][0].rearrange("(t p) d -> p t d", p=P)).then_inc(x_in, 16)
            sp.dma_start(table[:, :], consts_d).then_inc(const_in, 16)
            for u, unit in enumerate(units):
                if u >= RING1:
                    before = units[u - RING1]
                    sp.wait_ge(lo_done, before.first + before.quanta)
                sp.dma_start(slot(u % RING1)[:, 0:unit.size].rearrange("p (c n) -> p c n", c=unit.shape[0]),
                             unit.src).then_inc(loaded[u % RING1], 16)

            def source(kind, f, ex):
                if kind == "down":
                    return A["moe_wd"][0][ex][512 * f:512 * f + 512, :].rearrange("(c p) n -> p c n", p=P)
                return A["moe_wg" if kind == "gate" else "moe_wu"][0][ex][:, 512 * f:512 * f + 512].rearrange(
                    "(c p) n -> p c n", p=P)

            def load(j, i, ex, wait=True):
                kind, f = ORDER[j]
                if wait:
                    sp.wait_ge(lo_done, Q1 + QI * i + 4 * (j - RING2 + 1))
                c = 4 if kind == "down" else KC
                sp.dma_start(slot(j % RING2).rearrange("p (c n) -> p c n", c=c), source(kind, f, ex)).then_inc(
                    loaded[j % RING2], 16)

            for j in range(RING2):
                if j < RING1:
                    last = units[U1 - RING1 + j]
                    sp.wait_ge(lo_done, last.first + last.quanta)
                elif j == RING1:
                    sp.wait_ge(h_done, 4)
                load(j, 0, 0, wait=False)
            for j in range(RING2, UI):
                load(j, 0, 0)
            with sp.Fori(1, NE) as i:
                for j in range(UI):
                    load(j, i, i)
            sp.wait_ge(routed, 1)
            with sp.Fori(NE, ITEMS) as i:
                on = sp.value_load(active[0:1, bass.ds(i, 1)], min_val=0, max_val=1)
                with sp.If(on > 0):
                    ex = sp.value_load(expert[0:1, bass.ds(i, 1)], min_val=0, max_val=NE - 1)
                    for j in range(UI):
                        load(j, i, ex)
            for t in range(T):
                sp.wait_ge(out_ready, t + 1)
                sp.dma_start(out[0].rearrange("(t p) d -> p t d", p=P)[:, t], xn[:, t, :]).then_inc(stored, 16)
            sp.wait_ge(stored, 16 * T)

        @block.gpsimd
        def _(pool):
            def gains(*parts):
                at = 0
                for v, w in parts:
                    pool.dma_start(gain[:, at:at + w], v.partition_broadcast(P)).then_inc(gain_in, 16)
                    at += w
            gains((A["norm_mix_even"][0], D))
            for n, v in enumerate(("lam_q1", "lam_k1", "lam_q2", "lam_k2")):
                pool.dma_start(lamv[:, n, :], A[v][0].partition_broadcast(P)).then_inc(even_in, 16)
            pool.dma_start(sgu_w[:, :, :], A["sgu_w"][0].rearrange("g p q -> p g q")).then_inc(even_in, 16)
            with nc.allow_non_contiguous_dma("512 words, once"):
                pool.dma_start(sgu_b[:, :], A["sgu_b"][0].rearrange("g p -> p g")).then_inc(even_in, 16)
            pool.dma_start(subln[:, :], A["subln_g"][0].partition_broadcast(P)).then_inc(even_in, 16)
            pool.wait_ge(xn_done, 2)
            gains((A["sgu_ln_g"][0], 512), (A["sgu_ln_b"][0], 512))
            pool.wait_ge(even_in, 16 * 7)
            pool.affine_select(out=sgu_w[:, :, :], in_=sgu_w[:, :, :], compare_op=ALU.is_ge, fill=0.0, base=0,
                               pattern=[[0, 4], [-1, P]], channel_multiplier=1).then_inc(sgu_masked, 1)
            pool.wait_ge(ln_applied, 2)
            gains((A["norm_ffn_even"][0], D))
            pool.wait_ge(xn_done, 4)
            gains((A["norm_mix_odd"][0], D))
            pool.wait_ge(down_added, 2)
            pool.dma_start(bands, bands_d).then_inc(bands_in, 16)
            pool.dma_start(pool_w[:, :, :], A["pool_w"][0].rearrange("g c d -> c g d")).then_inc(odd_in, 16)
            with nc.allow_non_contiguous_dma("512 words, once"):
                pool.dma_start(pool_s[:, :], A["pool_scale"][0].rearrange("(g d) -> d g", d=P)).then_inc(odd_in, 16)
            pool.wait_ge(xn_done, 6)
            gains((A["q_norm_g"][0], CQ), (A["kv_norm_g"][0], CKV))
            pool.wait_ge(xn_done, 10)
            gains((A["norm_ffn_odd"][0], D))
            pool.wait_ge(h_done, 4)
            pool.dma_start(rw[:, :, :], A["router"][0].rearrange("(c p) n -> p c n", p=P)).then_inc(rw_in, 16)
            pool.wait_ge(xn_done, 12)
            gains((A["final_norm"], D))

        @block.scalar
        def _(act):
            chain = [0]
            split = [0]

            def link(ins):
                chain[0] += 1
                ins.then_inc(act_chain, 1)
                act.wait_ge(act_chain, chain[0])

            def hi_upto(n):
                while split[0] < min(n, Q1):
                    q = split[0]
                    u, k = quanta[q]
                    w = units[u].quantum
                    if k == 0:
                        act.wait_ge(loaded[u % RING1], 16 * (u // RING1 + 1))
                    if q >= NQ:
                        act.wait_ge(q_used, q - NQ + 1)
                    nc.scalar.activation(w_hi[:, q % NQ, 0:w], slot(u % RING1)[:, k * w:(k + 1) * w],
                                         ACT.Copy).then_inc(hi_done, 1)
                    split[0] += 1

            def ahead(u):
                hi_upto(units[u].first + units[u].quanta + NQ - 1)

            def norm_sums(n, srcs, junk):
                for c, src in enumerate(srcs):
                    nc.scalar.activation(junk[c], src, ACT.Square, accum_out=st("SSQ", c, 1)).then_inc(ssq_done, 1)

            def root(n, w):
                act.wait_ge(ms_done, n)
                nc.scalar.activation(st("ROOT", 0, w), st("MS", 0, w), ACT.Sqrt).then_inc(root_done, 1)

            def heads(name, dst, k0=0, count=4, chunks=2, base=0):
                for f in range(count):
                    k = fills[name] + f
                    act.wait_ge(*filled(k))
                    n = min(chunks, dst[1] - 2 * f)
                    nc.scalar.activation(dst[0][:, base + 2 * f:base + 2 * f + n, :],
                                         flat[:, 512 * (6 + k % 2):512 * (6 + k % 2) + 256 * n].rearrange(
                                             "p (c s) -> p c s", c=n), ACT.Copy).then_inc(t_head, 1)

            def block_psum(n, w):
                b = block_banks(n)
                return ps[:, b:b + 2, 0:w]

            def copy_block(u, dst, w, func=ACT.Copy):
                n = block_no[u]
                act.wait_ge(*used(u))
                return nc.scalar.activation(dst, block_psum(n, w), func).then_inc(blk_free[n % 2], 1)

            act.wait_ge(x_in, 16)
            norm_sums(0, [h[:, t, :] for t in range(T)], [xn[:, t, :] for t in range(T)])
            root(1, 2)
            hi_upto(NQ)
            heads("mix_even", (xt_hi, KC))
            g = groups["in_even"]
            for b in range(3):
                ahead(g[b])
                copy_block(g[b], proj[:, :, 512 * b:512 * b + 512], 512)
            ahead(g[3])
            copy_block(g[3], proj[:, :, 1536:2048], 512, ACT.Gelu_apprx_tanh)
            ahead(g[4])
            n = block_no[g[4]]
            act.wait_ge(*used(g[4]))
            for t in range(T):
                last = nc.scalar.activation(proj[:, t, 2048:2560], ps[:, block_banks(n) + t, :], ACT.Gelu_apprx_tanh,
                                            accum_out=st("SUM", t, 1))
            last.then_inc(blk_free[n % 2], 1)
            for t in range(T):
                if t == 0:
                    act.wait_ge(mu_done, 1)
                nc.scalar.activation(e[:, 2 * t:2 * t + 2, :], proj[:, t, 2048:2560].rearrange("p (a s) -> p a s", a=2),
                                     ACT.Square, bias=st("NEGMU", t, 1),
                                     accum_out=st("VSQ", t, 1)).then_inc(vsq_done, 1)
            root(2, 2)

            def evac_half(name, dst, count, parity):
                for f in range(count):
                    k = fills[name] + f
                    if k % 2 == parity:
                        act.wait_ge(*filled(k))
                        nc.scalar.activation(*dst(f, k), ACT.Copy).then_inc(t_free[k % 2], 1)

            def qk_fill(qt_, kt_, w):
                def at(f, k):
                    to = qt_ if f < 4 else kt_
                    m = 2 * (f % 4)
                    return (to[0:w, m:m + 2, :],
                            ps[0:w, 6 + k % 2, :].rearrange("p (m s) -> p m s", m=2))
                return at

            def pT_fill(et, qt):
                def at(f, k):
                    if qt == 0:
                        kt, m = 0, 4 * f
                    else:
                        kt, m = f // 2, 4 * (f % 2)
                    return et[:, kt, m:m + 4, :], ps[:, 6 + k % 2, :].rearrange("p (m s) -> p m s", m=4)
                return at

            def softmax(L, ee, et, name, qt):
                act.wait_ge(negmax, 2 * L + qt + 1)
                w = P * (qt + 1)
                for m in range(MAPS):
                    ins = nc.scalar.activation(ee[:, m, 0:w], ee[:, m, 0:w], ACT.Exp, bias=st("NEGMAX", m, 1),
                                               accum_out=st("ESUM", m, 1))
                ins.then_inc(exped, 1)
                base = name if qt == 0 else name + "1"
                evac_half(base, pT_fill(et, qt), 2 if qt == 0 else 4, 0)

            act.wait_ge(lam_dot, 1)
            nc.scalar.activation(st("LEXP"), st("LDOT"), ACT.Exp).then_inc(lam_exp, 1)
            evac_half("qk_a", qk_fill(qT, kT, A_QK), 8, 0)
            k = fills["sgu_w"]
            act.wait_ge(*filled(k))
            nc.scalar.activation(sgu_wT[:, :, :], ps[:, 6 + k % 2, :].rearrange("p (g q) -> p g q", g=4),
                                 ACT.Copy).then_inc(t_free[k % 2], 1)
            for qt in range(T):
                softmax(0, e, eT, "pT_a", qt)
            root(3, 8)
            heads("cat_even", (xt_hi, KC))
            for u in groups["out_even"]:
                ahead(u)
            act.wait_ge(h_done, 2)
            norm_sums(1, [h[:, t, :] for t in range(T)], [xn[:, t, :] for t in range(T)])
            root(4, 2)
            heads("ffn", (xt_hi, KC))
            for f, w in enumerate(widths):
                c = w // P
                ahead(groups["up"][f])
                act.wait_ge(*used(groups["up"][f]))
                silu_to = xn[:, 0, :].rearrange("p (c s) -> p c s", c=4)[:, 0:c, :]
                if f:
                    act.wait_ge(f_done, f)
                nc.scalar.activation(silu_to, ps[:, 0:c, 0:256], ACT.Silu).then_inc(fsilu, 1)
                act.wait_ge(fmul, f + 1)
                nc.scalar.activation(f_hi[:, f % 2, 0:c, :], silu_to, ACT.Copy).then_inc(f_head, 1)
            ahead(groups["down"][-1])
            act.wait_ge(down_added, 2)
            norm_sums(2, [h[:, t, :] for t in range(T)], [xn[:, t, :] for t in range(T)])
            root(5, 2)
            heads("mix_odd", (xt_hi, KC))
            for u, (c0, c1) in zip(groups["in_odd"], ((0, 512), (512, 512 + CQ), (512 + CQ, 1184))):
                ahead(u)
                copy_block(u, proj2[:, :, c0:c1], c1 - c0)
            n = block_no[groups["in_odd"][2]]
            act.wait_ge(*taken[n])
            act.wait_ge(*taken[n - 1])
            norm_sums(3, [proj2[:, t, 512:512 + CQ] for t in range(T)] + [proj2[:, t, 896:896 + CKV] for t in range(T)],
                      [xn[:, t, 0:CQ] for t in range(T)] + [xn[:, t, 512:512 + CKV] for t in range(T)])
            root(6, 4)
            for f in range(4):
                k = fills["pooled"] + f
                act.wait_ge(*filled(k))
                nc.scalar.activation(pooledT[:, f, :], ps[:, 6 + k % 2, 0:256], ACT.Copy).then_inc(t_free[k % 2], 1)
            for f in range(4):
                k = fills["poolout"] + f
                act.wait_ge(*filled(k))
                if f == 0:
                    act.wait_ge(odd_in, 32)
                nc.scalar.activation(xt_hi[:, f, :], ps[:, 6 + k % 2, 0:256], ACT.Copy,
                                     scale=pool_s[:, f:f + 1]).then_inc(t_head, 1)
            heads("cq", (c_hi, 3), count=2)
            heads("ckv", (c_hi, 2), count=1, base=3)
            for n, u in enumerate((groups["uq"][0], groups["ukv"][0])):
                ahead(u)
                act.wait_ge(*used(u))
                for t in range(T):
                    if n == 0:
                        ins = nc.scalar.activation(qf[:, t, :, :].rearrange("p m d -> p (m d)"),
                                                   flat[:, 1024 * t:1024 * t + 768], ACT.Copy)
                    else:
                        ins = nc.scalar.activation(kv[:, t, :, :].rearrange("p m d -> p (m d)"),
                                                   flat[:, 1024 * t:1024 * t + 1024], ACT.Copy)
                ins.then_inc(big_free, 1)
            evac_half("qk_d", qk_fill(qT2, kT2, D_QK), 8, 0)
            for qt in range(T):
                softmax(1, e2, eT2, "pT_d", qt)
            heads("cat_odd", (xt_hi, 8), count=2, base=4)
            for u in groups["out_odd"]:
                ahead(u)
            act.wait_ge(h_done, 4)
            norm_sums(4, [h[:, t, :] for t in range(T)], [xn[:, t, :] for t in range(T)])
            root(7, 2)
            for f in range(4):
                k = fills["router"] + f
                if k % 2 == 0:
                    act.wait_ge(*filled(k))
                    nc.scalar.activation(xT[:, 2 * f:2 * f + 2, :], ps[:, 6 + k % 2, :].rearrange("p (c s) -> p c s", c=2),
                                         ACT.Copy).then_inc(t_free[k % 2], 1)
            act.wait_ge(xn_done, 12)
            for t in range(T):
                nc.scalar.activation(xn_hi[:, t, :], xn[:, t, :], ACT.Copy).then_inc(xn_head, 1)
            act.wait_ge(top_done, 1)
            nc.scalar.activation(wts[:, :, 1:2], wts[:, :, 0:1], ACT.Exp).then_inc(top_exp, 1)
            assert split[0] == Q1
            act.wait_ge(routed, 1)
            with act.Fori(0, ITEMS) as i:
                on = act.value_load(active[0:1, bass.ds(i, 1)], min_val=0, max_val=1)
                with act.If(on > 0):
                    done = [0]

                    def heads_upto(n):
                        while done[0] < min(n, QI):
                            q = done[0]
                            j, k = q // 4, q % 4
                            if k == 0:
                                fills_before = U1 // RING1 if j % RING2 < RING1 else 0
                                act.wait_ge(loaded[j % RING2],
                                            16 * (fills_before + UI // RING2 * i + j // RING2 + 1))
                            act.wait_ge(q_used, Q1 + QI * i + q - NQ + 1)
                            nc.scalar.activation(w_hi[:, (Q1 + q) % NQ, :], slot(j % RING2)[:, 1024 * k:1024 * k + 1024],
                                                 ACT.Copy).then_inc(hi_done, 1)
                            done[0] += 1

                    def heads_ahead(unit):
                        heads_upto(4 * (pos_of[unit] + 1) + NQ - 1)

                    def hT_heads(f):
                        act.wait_ge(hT_ready, FB * i + f + 1)
                        nc.scalar.activation(hT_hi[:, :, :], ps[:, 7, :].rearrange("p (c s) -> p c s", c=4),
                                             ACT.Copy).then_inc(hT_head, 1)

                    heads_upto(NQ)
                    act.wait_ge(gathered, i + 1)
                    nc.scalar.activation(xg_hi[:, :, :], ps[:, 0:2, :].rearrange("p b (c s) -> p (b c) s", s=P),
                                         ACT.Copy).then_inc(xg_head, 1)
                    act.wait_ge(pickT_ready, i + 1)
                    nc.scalar.activation(pickT[:, :], ps[:, 6, 0:S], ACT.Copy).then_inc(pickT_done, 1)
                    for f in range(FB):
                        if f:
                            heads_ahead(("gate", f))
                            hT_heads(f - 1)
                        heads_ahead(("up", f))
                        act.wait_ge(q_used, Q1 + QI * i + 4 * (pos_of[("up", f)] + 1))
                        if f:
                            act.wait_ge(mul_done, FB * i + f)
                        nc.scalar.activation(g_act, ps[:, 2 * (f % 2), :], ACT.Silu).then_inc(silu_done, 1)
                    heads_ahead(("down", FB - 2))
                    hT_heads(FB - 1)
                    heads_upto(QI)
                    act.wait_ge(q_used, Q1 + QI * (i + 1))
                    nc.scalar.activation(y_hi[:, :], flat[:, 2048:3072], ACT.Copy).then_inc(y_head, 1)
            act.wait_ge(experts_done, 1)
            norm_sums(5, [h[:, t, :] for t in range(T)], [xn[:, t, :] for t in range(T)])
            root(8, 2)

        @block.vector
        def _(dve):
            chain = [0]
            split = [0]
            v = nc.vector

            def link(ins):
                chain[0] += 1
                ins.then_inc(dve_chain, 1)
                dve.wait_ge(dve_chain, chain[0])

            def lo_upto(n):
                while split[0] < min(n, Q1):
                    q = split[0]
                    u, k = quanta[q]
                    w = units[u].quantum
                    dve.wait_ge(hi_done, q + 1)
                    v.tensor_tensor(w_lo[:, q % NQ, 0:w], slot(u % RING1)[:, k * w:(k + 1) * w],
                                    w_hi[:, q % NQ, 0:w].bitcast(F32), ALU.subtract).then_inc(lo_done, 1)
                    split[0] += 1

            def ahead(u):
                lo_upto(units[u].first + units[u].quanta + NQ - 1)

            ssq = [0]
            gains = [0]

            def mean_eps(w, width, eps=NORM_EPS, src="SSQ"):
                v.tensor_scalar(st("MS", 0, w), st(src, 0, w), 1.0 / width, eps, ALU.mult, ALU.add).then_inc(ms_done, 1)

            def inverse(n, w):
                dve.wait_ge(root_done, n)
                link(v.reciprocal(st("ROOT", 0, w), st("ROOT", 0, w)))

            def rmsnorm(n, gain_count):
                ssq[0] += 2
                dve.wait_ge(ssq_done, ssq[0])
                mean_eps(2, D)
                inverse(n, 2)
                dve.wait_ge(gain_in, 16 * gain_count)
                for t in range(T):
                    v.scalar_tensor_tensor(out=xn[:, t, :], in0=h[:, t, :], scalar=st("ROOT", t, 1),
                                           in1=gain[:, :], op0=ALU.mult, op1=ALU.mult).then_inc(xn_done, 1)

            heads_seen = [0]

            def rests(name, dst, count=4, base=0):
                for f in range(count):
                    k = fills[name] + f
                    n = min(2, dst[2] - 2 * f)
                    heads_seen[0] += 1
                    dve.wait_ge(t_head, heads_seen[0])
                    v.tensor_tensor(dst[1][:, base + 2 * f:base + 2 * f + n, :],
                                    flat[:, 512 * (6 + k % 2):512 * (6 + k % 2) + 256 * n].rearrange(
                                        "p (c s) -> p c s", c=n),
                                    dst[0][:, base + 2 * f:base + 2 * f + n, :].bitcast(F32),
                                    ALU.subtract).then_inc(t_free[k % 2], 1)

            def rope(x, tab, half, G, tmp):
                a, _ = CONST[tab]
                cs = [table[:, a + n * T * half:a + (n + 1) * T * half].rearrange("p (t u k) -> p t u k", t=T, u=1)
                      .to_broadcast([P, T, G, half]) for n in range(2)]
                x1, x2 = x[:, :, :, 0:half], x[:, :, :, half:2 * half]
                v.tensor_tensor(tmp[0], x1, cs[0], ALU.mult)
                v.tensor_tensor(tmp[1], x2, cs[1], ALU.mult)
                v.tensor_tensor(tmp[2], x2, cs[0], ALU.mult)
                link(v.tensor_tensor(tmp[3], x1, cs[1], ALU.mult))
                v.tensor_tensor(x1, tmp[0], tmp[1], ALU.subtract)
                return v.tensor_tensor(x2, tmp[2], tmp[3], ALU.add)

            def scratch(buf, G, half):
                f = buf[:, :, :].rearrange("p m s -> p (m s)")
                w = T * G * half
                return [f[:, n * w:(n + 1) * w].rearrange("p (t g k) -> p t g k", t=T, g=G) for n in range(4)]

            def evac_half(name, dst, count, parity):
                for f in range(count):
                    k = fills[name] + f
                    if k % 2 == parity:
                        dve.wait_ge(*filled(k))
                        v.tensor_copy(*dst(f, k)).then_inc(t_free[k % 2], 1)

            def qk_fill(qt_, kt_, w):
                def at(f, k):
                    to = qt_ if f < 4 else kt_
                    m = 2 * (f % 4)
                    return (to[0:w, m:m + 2, :],
                            ps[0:w, 6 + k % 2, :].rearrange("p (m s) -> p m s", m=2))
                return at

            def pT_fill(et, qt):
                def at(f, k):
                    if qt == 0:
                        kt, m = 0, 4 * f
                    else:
                        kt, m = f // 2, 4 * (f % 2)
                    return et[:, kt, m:m + 4, :], ps[:, 6 + k % 2, :].rearrange("p (m s) -> p m s", m=4)
                return at

            causal = con("causal").rearrange("p (u k) -> p u k", u=1).to_broadcast([P, MAPS, P])

            def scores(L, ee, scale, qt):
                dve.wait_ge(scored, 2 * L + qt + 1)
                if qt == 0:
                    link(v.scalar_tensor_tensor(out=ee[:, :, 0:P], in0=ps[:, 4:6, :].rearrange("p b (m k) -> p (b m) k", k=P),
                                                scalar=scale, in1=causal, op0=ALU.mult, op1=ALU.add))
                else:
                    k = fills["pT_a" if L == 0 else "pT_d"]
                    dve.wait_ge(*filled(k))
                    dve.wait_ge(*filled(k + 1))
                    sc = ps[:, 0:4, :].rearrange("p b (m k) -> p (b m) k", k=S)
                    v.tensor_scalar(ee[:, :, 0:P], sc[:, :, 0:P], scale, None, ALU.mult)
                    link(v.scalar_tensor_tensor(out=ee[:, :, P:S], in0=sc[:, :, P:S], scalar=scale, in1=causal,
                                                op0=ALU.mult, op1=ALU.add))
                link(v.reduce_max(st("MAX"), ee[:, :, 0:P * (qt + 1)], AX.X))
                v.tensor_scalar(st("NEGMAX"), st("MAX"), -1.0, None, ALU.mult).then_inc(negmax, 1)

            def sums(L, qt):
                dve.wait_ge(exped, 2 * L + qt + 1)
                link(v.reciprocal(st("EINV"), st("ESUM")))

            dve.wait_ge(const_in, 16)
            rmsnorm(1, 1)
            lo_upto(NQ)
            rests("mix_even", (xt_hi, xt_lo, KC))
            g = groups["in_even"]
            ahead(g[0])
            dve.wait_ge(even_in, 16 * 7)
            for n in range(2):
                ins = v.tensor_tensor_reduce(out=lamj[:, n, :], in0=lamv[:, 2 * n, :], in1=lamv[:, 2 * n + 1, :], scale=1.0,
                                             scalar=0.0, op0=ALU.mult, op1=ALU.add, accum_out=st("LDOT", n, 1))
            ins.then_inc(lam_dot, 1)
            ahead(g[1])
            n = block_no[g[1]]
            dve.wait_ge(*taken[n])
            dve.wait_ge(*taken[n - 1])
            rope(proj[:, :, 0:1024].rearrange("p t (g k) -> p t g k", g=16)[:, :, :, 0:16], "ropeA", A_HALF, 16,
                 scratch(e, 16, A_HALF)).then_inc(roped, 1)
            for b in range(2, 5):
                ahead(g[b])
            n = block_no[g[4]]
            dve.wait_ge(*taken[n])
            v.tensor_scalar(st("NEGMU"), st("SUM"), -1.0 / 512, None, ALU.mult).then_inc(mu_done, 1)
            dve.wait_ge(vsq_done, 2)
            mean_eps(2, 512, LN_EPS, "VSQ")
            evac_half("qk_a", qk_fill(qT, kT, A_QK), 8, 1)
            inverse(2, 2)
            dve.wait_ge(gain_in, 16 * 3)
            vg = proj[:, :, 2048:2560]
            for t in range(T):
                link(v.scalar_tensor_tensor(out=vg[:, t, :], in0=vg[:, t, :], scalar=st("NEGMU", t, 1),
                                            in1=gain[:, 0:512], op0=ALU.add, op1=ALU.mult))
                v.scalar_tensor_tensor(out=vg[:, t, :], in0=vg[:, t, :], scalar=st("ROOT", t, 1),
                                       in1=gain[:, 512:1024], op0=ALU.mult, op1=ALU.add).then_inc(ln_applied, 1)
            dve.wait_ge(lam_exp, 1)
            link(v.tensor_tensor(st("NLAM"), st("LEXP", 1, 1), st("LEXP", 0, 1), ALU.subtract))
            link(v.tensor_scalar(st("NLAM"), st("NLAM"), LAM_INIT, None, ALU.subtract))
            scores(0, e, A_SCALE, 0)
            for f in range(2):
                k = fills["mixed"] + f
                dve.wait_ge(*filled(k))
                for gr in range(4):
                    ub = proj[:, f, 1536 + P * gr:1536 + P * (gr + 1)]
                    ins = v.scalar_tensor_tensor(out=ub, in0=ps[:, 6 + k % 2, P * gr:P * (gr + 1)],
                                                 scalar=sgu_b[:, gr:gr + 1], in1=ub, op0=ALU.add, op1=ALU.mult)
                ins.then_inc(t_free[k % 2], 1)
            oa = proj[:, :, 0:512].rearrange("p t (m d) -> p t m d", m=4)
            for qt in range(T):
                if qt:
                    scores(0, e, A_SCALE, 1)
                sums(0, qt)
                link(v.tensor_scalar(st("EINV", 4, 4), st("EINV", 4, 4), st("NLAM"), None, ALU.mult))
                evac_half("pT_a" if qt == 0 else "pT_a1", pT_fill(eT, qt), 2 if qt == 0 else 4, 1)
                dve.wait_ge(o_ready, qt + 1)
                for j in range(2):
                    r = st("EINV", 4 * j, 4).rearrange("p (m u) -> p m u", u=1).to_broadcast([P, 4, P])
                    dst = oa[:, qt] if j == 0 else proj[:, qt, 512:1024].rearrange("p (m d) -> p m d", m=4)
                    ins = v.tensor_tensor(dst, ps[:, 4 + j, :].rearrange("p (m d) -> p m d", m=4), r, ALU.mult)
                ins.then_inc(o_free, 1)
                dve.wait_ge(o_free, qt + 1)
                link(v.tensor_tensor(proj[:, qt, 0:512], proj[:, qt, 0:512], proj[:, qt, 512:1024], ALU.add))
            link(v.tensor_tensor(proj[:, :, 512:1024], proj[:, :, 0:512], proj[:, :, 0:512], ALU.mult))
            link(v.reduce_sum(st("SSQ"), proj[:, :, 512:1024].rearrange("p t (m d) -> p t m d", m=4), AX.X))
            mean_eps(8, P)
            inverse(3, 8)
            sb = subln[:, :].rearrange("p (u d) -> p u d", u=1).to_broadcast([P, 4, P])
            for t in range(T):
                r = st("ROOT", 4 * t, 4).rearrange("p (m u) -> p m u", u=1).to_broadcast([P, 4, P])
                link(v.tensor_tensor(oa[:, t], oa[:, t], r, ALU.mult))
                v.scalar_tensor_tensor(out=oa[:, t], in0=oa[:, t], scalar=1.0 - LAM_INIT, in1=sb, op0=ALU.mult,
                                       op1=ALU.mult).then_inc(oa_done, 1)
            rests("cat_even", (xt_hi, xt_lo, KC))

            def residual(u, b):
                ahead(u)
                n = block_no[u]
                dve.wait_ge(*used(u))
                hb = h[:, :, 512 * b:512 * b + 512]
                v.tensor_tensor(hb, hb, ps[:, block_banks(n):block_banks(n) + 2, :], ALU.add).then_inc(h_done, 1)

            for b, u in enumerate(groups["out_even"]):
                residual(u, b)
            dve.wait_ge(h_done, 2)
            rmsnorm(4, 4)
            rests("ffn", (xt_hi, xt_lo, KC))
            for f, w in enumerate(widths):
                c = w // P
                ahead(groups["up"][f])
                dve.wait_ge(fsilu, f + 1)
                x = xn[:, 0, :].rearrange("p (c s) -> p c s", c=4)[:, 0:c, :]
                v.tensor_tensor(x, x, ps[:, 0:c, 256:512], ALU.mult).then_inc(fmul, 1)
                dve.wait_ge(f_head, f + 1)
                v.tensor_tensor(f_lo[:, f % 2, 0:c, :], x, f_hi[:, f % 2, 0:c, :].bitcast(F32),
                                ALU.subtract).then_inc(f_done, 1)
            ahead(groups["down"][-1])
            dve.wait_ge(*used(groups["down"][-1]))
            for t in range(T):
                v.tensor_tensor(h[:, t, :], h[:, t, :], flat[:, 2048 + 1024 * t:3072 + 1024 * t],
                                ALU.add).then_inc(down_added, 1)
            dve.wait_ge(down_added, 2)
            rmsnorm(5, 5)
            rests("mix_odd", (xt_hi, xt_lo, KC))
            for u in groups["in_odd"]:
                ahead(u)
            ssq[0] += 4
            dve.wait_ge(ssq_done, ssq[0])
            v.tensor_scalar(st("MS", 0, 2), st("SSQ", 0, 2), 1.0 / CQ, NORM_EPS, ALU.mult, ALU.add)
            v.tensor_scalar(st("MS", 2, 2), st("SSQ", 2, 2), 1.0 / CKV, NORM_EPS, ALU.mult, ALU.add).then_inc(ms_done, 1)
            kpe = proj2[:, :, 1152:1184].rearrange("p t (u k) -> p t u k", u=1)
            link(rope(kpe, "ropeD", D_HALF, 1, [xn[:, :, 768 + 16 * n:784 + 16 * n].rearrange("p t (u k) -> p t u k", u=1)
                                                for n in range(4)]))
            inverse(6, 4)
            dve.wait_ge(gain_in, 16 * 7)
            for n, (a, b, ga) in enumerate(((512, 896, 0), (896, 1152, CQ))):
                for t in range(T):
                    v.scalar_tensor_tensor(out=proj2[:, t, a:b], in0=proj2[:, t, a:b],
                                           scalar=st("ROOT", 2 * n + t, 1), in1=gain[:, ga:ga + b - a],
                                           op0=ALU.mult, op1=ALU.mult).then_inc(xn_done, 1)
            for f in range(4):
                k = fills["poolout"] + f
                heads_seen[0] += 1
                dve.wait_ge(t_head, heads_seen[0])
                v.scalar_tensor_tensor(out=xt_lo[:, f, :], in0=ps[:, 6 + k % 2, 0:256], scalar=pool_s[:, f:f + 1],
                                       in1=xt_hi[:, f, :].bitcast(F32), op0=ALU.mult,
                                       op1=ALU.subtract).then_inc(t_free[k % 2], 1)
            rests("cq", (c_hi, c_lo, 3), count=2)
            rests("ckv", (c_hi, c_lo, 2), count=1, base=3)
            ahead(groups["uq"][0])
            dve.wait_ge(big_free, 1)
            link(rope(qf[:, :, :, D_NOPE:D_QK], "ropeD", D_HALF, MAPS, scratch(e2, MAPS, D_HALF)))
            ahead(groups["ukv"][0])
            v.tensor_copy(kf[:, :, :, D_NOPE:D_QK], kpe.to_broadcast([P, T, MAPS, 2 * D_HALF]))
            dve.wait_ge(big_free, 2)
            v.tensor_copy(kf[:, :, :, 0:D_NOPE], kv[:, :, :, 0:D_NOPE]).then_inc(kf_done, 1)
            evac_half("qk_d", qk_fill(qT2, kT2, D_QK), 8, 1)
            for qt in range(T):
                scores(1, e2, D_SCALE, qt)
                sums(1, qt)
                evac_half("pT_d" if qt == 0 else "pT_d1", pT_fill(eT2, qt), 2 if qt == 0 else 4, 1)
                dve.wait_ge(o_ready, 3 + qt)
                r = st("EINV").rearrange("p (m u) -> p m u", u=1).to_broadcast([P, MAPS, D_V])
                v.tensor_tensor(proj2[:, qt, 0:512].rearrange("p (m d) -> p m d", m=MAPS),
                                ps[:, 4, :].rearrange("p (m d) -> p m d", m=MAPS), r, ALU.mult).then_inc(o_free, 1)
            rests("cat_odd", (xt_hi, xt_lo, 8), count=2, base=4)
            for b, u in enumerate(groups["out_odd"]):
                residual(u, b)
            dve.wait_ge(h_done, 4)
            rmsnorm(7, 8)
            for f in range(4):
                k = fills["router"] + f
                if k % 2 == 1:
                    dve.wait_ge(*filled(k))
                    v.tensor_copy(xT[:, 2 * f:2 * f + 2, :], ps[:, 6 + k % 2, :].rearrange("p (c s) -> p c s", c=2)).then_inc(
                        t_free[k % 2], 1)
            for t in range(T):
                dve.wait_ge(xn_head, t + 1)
                v.tensor_tensor(xn_lo[:, t, :], xn[:, t, :], xn_hi[:, t, :].bitcast(F32), ALU.subtract).then_inc(xn_rest, 1)
            k = fills["logits"]
            dve.wait_ge(*filled(k))
            v.tensor_copy(lg[:, :, :], ps[:, 6 + k % 2, 0:T * NE].rearrange("p (t n) -> p t n", t=T)).then_inc(t_free[k % 2], 1)
            dve.wait_ge(*emptied(k))
            for t in range(T):
                ins = v.max(top[:, t, :], lg[:, t, :])
            link(ins)
            v.tensor_tensor(wts[:, :, 0:1], top[:, :, 1:2], top[:, :, 0:1], ALU.subtract).then_inc(top_done, 1)
            lower = con("lower8").rearrange("p (a b) -> p a b", a=NE)
            for t in range(T):
                mine = lg[:, t, :].rearrange("p (a u) -> p a u", u=1).to_broadcast([P, NE, NE])
                other = lg[:, t, :].rearrange("p (u b) -> p u b", u=1).to_broadcast([P, NE, NE])
                v.tensor_tensor(cmp1[:, t], other, mine, ALU.is_gt)
                link(v.tensor_tensor(cmp2[:, t], other, mine, ALU.is_equal))
                link(v.tensor_tensor(cmp2[:, t], cmp2[:, t], lower, ALU.mult))
                link(v.tensor_tensor(cmp1[:, t], cmp1[:, t], cmp2[:, t], ALU.add))
            link(v.reduce_sum(rank[:, :, :], cmp1[:, :, :, :], AX.X))
            v.tensor_scalar(sel[:, :, :], rank[:, :, :], 2.0, None, ALU.is_lt).then_inc(sel_done, 1)
            dve.wait_ge(top_exp, 1)
            link(v.tensor_scalar(wts[:, :, 2:3], wts[:, :, 1:2], 1.0, None, ALU.add))
            link(v.reciprocal(wts[:, :, 2:3], wts[:, :, 2:3]))
            link(v.tensor_tensor(wts[:, :, 3:4], wts[:, :, 1:2], wts[:, :, 2:3], ALU.mult))
            for n in range(2):
                link(v.tensor_scalar(gtmp[:, :, :], rank[:, :, :], float(n), None, ALU.is_equal))
                dst = gate if n == 0 else gtmp
                link(v.tensor_tensor(dst[:, :, :], gtmp[:, :, :], wts[:, :, 2 + n:3 + n].to_broadcast([P, T, NE]), ALU.mult))
            link(v.tensor_tensor(gate[:, :, :], gate[:, :, :], gtmp[:, :, :], ALU.add))
            k = fills["prefix"]
            dve.wait_ge(*filled(k))
            v.tensor_copy(over[:, 3, :], ps[:, 6 + k % 2, 16:24])
            link(v.tensor_scalar(place[:, :, :], ps[:, 6 + k % 2, 0:T * NE].rearrange("p (t n) -> p t n", t=T), 1.0, None,
                                 ALU.add))
            link(v.tensor_tensor(place[:, :, :], place[:, :, :], sel[:, :, :], ALU.mult))
            link(v.tensor_scalar(place[:, :, :], place[:, :, :], -1.0, None, ALU.add))
            v.tensor_copy(slot_of[:, :, 0:NE], place[:, :, :])
            v.tensor_copy(gate_of[:, :, 0:NE], gate[:, :, :])
            v.memset(active[0:1, 0:NE], 1)
            link(v.memset(expert[0:1, 0:NE], 0))
            link(v.tensor_scalar(over[:, 0, :], over[:, 3, :], float(SLOTS), None, ALU.is_gt))
            o_row = over[:, 0, :].rearrange("p (u b) -> p u b", u=1).to_broadcast([P, NE, NE])
            link(v.tensor_tensor(cmp1[:, 0], o_row, lower, ALU.mult))
            link(v.reduce_sum(over[:, 1, :], cmp1[:, 0], AX.X))
            link(v.tensor_scalar(place[:, :, :], place[:, :, :], -float(SLOTS), None, ALU.add))
            for x in range(EXTRA):
                link(v.tensor_scalar(over[:, 2, :], over[:, 1, :], float(x), None, ALU.is_equal))
                link(v.tensor_tensor(over[:, 2, :], over[:, 2, :], over[:, 0, :], ALU.mult))
                link(v.reduce_sum(st("TMP"), over[:, 2, :], AX.X))
                link(v.tensor_copy(active[0:1, NE + x:NE + x + 1], st("TMP")[0:1, :]))
                link(v.tensor_tensor(over[:, 3, :], over[:, 2, :], con("iota8"), ALU.mult))
                link(v.reduce_sum(st("TMP"), over[:, 3, :], AX.X))
                link(v.tensor_copy(expert[0:1, NE + x:NE + x + 1], st("TMP")[0:1, :]))
                one = over[:, 2, :].rearrange("p (u b) -> p u b", u=1).to_broadcast([P, T, NE])
                for src, dst in ((place, slot_of), (gate, gate_of)):
                    link(v.tensor_tensor(gtmp[:, :, :], src[:, :, :], one, ALU.mult))
                    link(v.reduce_sum(dst[:, :, NE + x], gtmp[:, :, :], AX.X))
            v.memset(st("JUNK"), 0.0).then_inc(routed, 1)
            dve.wait_ge(routed, 1)
            with dve.Fori(0, ITEMS) as i:
                on = dve.value_load(active[0:1, bass.ds(i, 1)], min_val=0, max_val=1)
                with dve.If(on > 0):
                    done = [0]

                    def rests_upto(n):
                        while done[0] < min(n, QI):
                            q = done[0]
                            j, k = q // 4, q % 4
                            dve.wait_ge(hi_done, Q1 + QI * i + q + 1)
                            v.tensor_tensor(w_lo[:, (Q1 + q) % NQ, :], slot(j % RING2)[:, 1024 * k:1024 * k + 1024],
                                            w_hi[:, (Q1 + q) % NQ, :].bitcast(F32), ALU.subtract).then_inc(lo_done, 1)
                            done[0] += 1

                    def rests_ahead(unit):
                        rests_upto(4 * (pos_of[unit] + 1) + NQ - 1)

                    def hT_rests(f):
                        dve.wait_ge(hT_head, FB * i + f + 1)
                        v.tensor_tensor(hT_lo[:, :, :], ps[:, 7, :].rearrange("p (c s) -> p c s", c=4),
                                        hT_hi[:, :, :].bitcast(F32), ALU.subtract).then_inc(hT_rest, 1)

                    for t in range(T):
                        ins = v.tensor_scalar(pick[:, t, :], con("iota"), slot_of[:, t, bass.ds(i, 1)], None, ALU.is_equal)
                    ins.then_inc(picked, 1)
                    rests_upto(NQ)
                    dve.wait_ge(gathered, i + 1)
                    v.tensor_copy(xg_lo[:, :, :], ps[:, 2:4, :].rearrange("p b (c s) -> p (b c) s", s=P)).then_inc(xg_rest, 1)
                    for f in range(FB):
                        if f:
                            rests_ahead(("gate", f))
                            hT_rests(f - 1)
                        rests_ahead(("up", f))
                        dve.wait_ge(silu_done, FB * i + f + 1)
                        if f:
                            dve.wait_ge(hT_ready, FB * i + f)
                        v.tensor_tensor(g_mul, g_act, ps[:, 2 * (f % 2) + 1, :], ALU.mult).then_inc(mul_done, 1)
                    rests_ahead(("down", FB - 2))
                    hT_rests(FB - 1)
                    rests_upto(QI)
                    dve.wait_ge(y_head, i + 1)
                    v.tensor_tensor(y_lo[:, :], flat[:, 2048:3072], y_hi[:, :].bitcast(F32), ALU.subtract).then_inc(y_rest, 1)
                    dve.wait_ge(scattered, i + 1)
                    for t in range(T):
                        v.scalar_tensor_tensor(out=h[:, t, :], in0=flat[:, 1024 * t:1024 * t + 1024],
                                               scalar=gate_of[:, t, bass.ds(i, 1)], in1=h[:, t, :],
                                               op0=ALU.mult, op1=ALU.add).then_inc(added, 1)
                    dve.wait_ge(added, 2 * i + 2)
                    v.memset(st("MARK"), 0.0)
            v.memset(st("JUNK"), 0.0).then_inc(experts_done, 1)
            ssq[0] += 2
            dve.wait_ge(ssq_done, ssq[0])
            mean_eps(2, D)
            inverse(8, 2)
            dve.wait_ge(gain_in, 16 * 9)
            for t in range(T):
                v.scalar_tensor_tensor(out=xn[:, t, :], in0=h[:, t, :], scalar=st("ROOT", t, 1),
                                       in1=gain[:, :], op0=ALU.mult, op1=ALU.mult).then_inc(out_ready, 1)

        @block.tensor
        def _(pe):
            def bank_free(k):
                if k >= 2:
                    pe.wait_ge(*emptied(k - 2))

            def three(out_, a_hi, a_lo, q, c0, c1, first, last):
                pe.matmul(out_, a_hi, w_hi[:, q, c0:c1], start=first, stop=False)
                pe.matmul(out_, a_hi, w_lo[:, q, c0:c1], start=False, stop=False)
                return pe.matmul(out_, a_lo, w_hi[:, q, c0:c1], start=False, stop=last)

            def transposes(name, src, chunks, wait=None):
                for f in range((chunks + 1) // 2):
                    k = fills[name] + f
                    bank_free(k)
                    for c in range(2 * f, min(2 * f + 2, chunks)):
                        for t in range(T):
                            ins = pe.transpose(ps[:, 6 + k % 2, 256 * (c % 2) + P * t:256 * (c % 2) + P * (t + 1)],
                                               src(c, t), ident)
                    ins.then_inc(t_ready[k % 2], 1)

            def ready_after(name, chunk):
                pe.wait_ge(*emptied(fills[name] + chunk // 2))

            def attention(name, qt_, kt_, w, src_q, src_k):
                for f in range(8):
                    k = fills["qk_" + name] + f
                    bank_free(k)
                    src = src_q if f < 4 else src_k
                    for mm in range(2):
                        m = 2 * (f % 4) + mm
                        for t in range(T):
                            ins = pe.transpose(ps[0:w, 6 + k % 2, 256 * mm + P * t:256 * mm + P * (t + 1)], src(m, t), ident)
                    ins.then_inc(t_ready[k % 2], 1)
                pe.wait_ge(*emptied(fills["qk_" + name] + 6))
                pe.wait_ge(*emptied(fills["qk_" + name] + 7))
                for m in range(MAPS):
                    ins = pe.matmul(ps[:, 4 + m // 4, P * (m % 4):P * (m % 4 + 1)], qt_[0:w, m, 0:P], kt_[0:w, m, 0:P],
                                    start=True, stop=True)
                ins.then_inc(scored, 1)
                if name == "a":
                    n = block_no[groups["in_even"][-1]]
                    pe.wait_ge(*taken[n])
                    pe.wait_ge(*taken[n - 1])
                for m in range(MAPS):
                    ins = pe.matmul(ps[:, m // 2, S * (m % 2):S * (m % 2 + 1)], qt_[0:w, m, P:S], kt_[0:w, m, :],
                                    start=True, stop=True)
                ins.then_inc(scored, 1)

            def values(L, name, ee, et, value, dv, qt):
                pe.wait_ge(exped, 2 * L + qt + 1)
                n = 2 if qt == 0 else 4
                base = fills["pT_" + name] + (0 if qt == 0 else 2)
                for f in range(n):
                    k = base + f
                    bank_free(k)
                    kt, m0 = (0, 4 * f) if qt == 0 else (f // 2, 4 * (f % 2))
                    for m in range(4):
                        ins = pe.transpose(ps[:, 6 + k % 2, P * m:P * (m + 1)], ee[:, m0 + m, P * kt:P * (kt + 1)], ident)
                    ins.then_inc(t_ready[k % 2], 1)
                pe.wait_ge(*emptied(base + n - 2))
                pe.wait_ge(*emptied(base + n - 1))
                if qt or L:
                    pe.wait_ge(o_free, 2 * L + qt)
                for m in range(MAPS):
                    o = flat[:, 2048 + dv * m:2048 + dv * (m + 1)]
                    for kt in range(qt + 1):
                        ins = pe.matmul(o, et[:, kt, m, :], value(m, kt), start=(kt == 0), stop=(kt == qt))
                ins.then_inc(o_ready, 1)

            pe.wait_ge(const_in, 16)
            pe.wait_ge(xn_done, 2)
            transposes("mix_even", lambda c, t: xn[:, t, P * c:P * (c + 1)], KC)

            def run_block(u, name):
                n, unit = block_no[u], units[u]
                if n >= 2:
                    pe.wait_ge(*taken[n - 2])
                w = unit.shape[1]
                for kq in range(unit.quanta):
                    q = unit.first + kq
                    pe.wait_ge(lo_done, q + 1)
                    if name:
                        ready_after(name, 2 * kq)
                    for t in range(T):
                        for c in range(2):
                            kc = 2 * kq + c
                            ins = three(ps[:, block_banks(n) + t, 0:w], xt_hi[:, kc, P * t:P * (t + 1)],
                                        xt_lo[:, kc, P * t:P * (t + 1)], q % NQ, c * w, (c + 1) * w,
                                        kc == 0, kc == KC - 1)
                    ins.then_inc(q_used, 1)

            for b, u in enumerate(groups["in_even"]):
                run_block(u, "mix_even" if b == 0 else None)
            pe.wait_ge(roped, 1)
            attention("a", qT, kT, A_QK,
                      lambda m, t: proj[:, t, (m % 4) * P + 64 * (m // 4):(m % 4) * P + 64 * (m // 4) + 64],
                      lambda m, t: proj[:, t, 512 + (m % 4) * P + 64 * (m // 4):512 + (m % 4) * P + 64 * (m // 4) + 64])
            k = fills["sgu_w"]
            bank_free(k)
            pe.wait_ge(sgu_masked, 1)
            for gr in range(4):
                ins = pe.transpose(ps[:, 6 + k % 2, P * gr:P * (gr + 1)], sgu_w[:, gr, :], ident)
            ins.then_inc(t_ready[k % 2], 1)
            pe.wait_ge(*emptied(k))
            for f in range(2):
                k = fills["mixed"] + f
                bank_free(k)
                pe.wait_ge(ln_applied, 2)
                for gr in range(4):
                    ins = pe.matmul(ps[:, 6 + k % 2, P * gr:P * (gr + 1)], sgu_wT[:, gr, :],
                                    proj[:, f, 2048 + P * gr:2048 + P * (gr + 1)], start=True, stop=True)
                ins.then_inc(t_ready[k % 2], 1)
            for qt in range(T):
                values(0, "a", e, eT, lambda m, kt: proj[:, kt, 1024 + P * (m % 4):1024 + P * (m % 4 + 1)], P, qt)
            pe.wait_ge(oa_done, 2)
            transposes("cat_even", lambda c, t: proj[:, t, P * c:P * (c + 1)] if c < 4 else
                       proj[:, t, 1536 + P * (c - 4):1536 + P * (c - 3)], KC)
            for b, u in enumerate(groups["out_even"]):
                run_block(u, "cat_even" if b == 0 else None)
            pe.wait_ge(xn_done, 4)
            transposes("ffn", lambda c, t: xn[:, t, P * c:P * (c + 1)], KC)

            def ffn_down(f):
                unit = units[groups["down"][f]]
                pe.wait_ge(f_done, f + 1)
                for c in range(unit.quanta):
                    q = unit.first + c
                    pe.wait_ge(lo_done, q + 1)
                    for t in range(T):
                        for half in range(2):
                            ins = three(ps[:, 4 + 2 * t + half, :], f_hi[:, f % 2, c, P * t:P * (t + 1)],
                                        f_lo[:, f % 2, c, P * t:P * (t + 1)], q % NQ, 512 * half, 512 * half + 512,
                                        f == 0 and c == 0, f == len(widths) - 1 and c == unit.quanta - 1)
                    ins.then_inc(q_used, 1)

            for f, w in enumerate(widths):
                nch = w // P
                if f:
                    pe.wait_ge(fmul, f)
                else:
                    pe.wait_ge(h_done, 2)
                for part, name in enumerate(("gate", "up")):
                    unit = units[groups[name][f]]
                    per = KC // unit.quanta
                    for kq in range(unit.quanta):
                        q = unit.first + kq
                        pe.wait_ge(lo_done, q + 1)
                        for c in range(per):
                            kc = kq * per + c
                            if f == 0 and part == 0 and kc % 2 == 0:
                                ready_after("ffn", kc)
                            for fc in range(nch):
                                o = ps[:, fc, 256 * part:256 * part + 256]
                                a, b = c * w + P * fc, c * w + P * (fc + 1)
                                pe.matmul(o, w_hi[:, q % NQ, a:b], xt_hi[:, kc, :], start=(kc == 0), stop=False)
                                pe.matmul(o, w_hi[:, q % NQ, a:b], xt_lo[:, kc, :], start=False, stop=False)
                                ins = pe.matmul(o, w_lo[:, q % NQ, a:b], xt_hi[:, kc, :], start=False, stop=(kc == KC - 1))
                        ins.then_inc(q_used, 1)
                if f:
                    ffn_down(f - 1)
            ffn_down(len(widths) - 1)
            pe.wait_ge(xn_done, 6)
            transposes("mix_odd", lambda c, t: xn[:, t, P * c:P * (c + 1)], KC)
            for b, u in enumerate(groups["in_odd"]):
                run_block(u, "mix_odd" if b == 0 else None)
            n = block_no[groups["in_odd"][0]]
            pe.wait_ge(*taken[n])
            pe.wait_ge(bands_in, 16)
            for gr in range(4):
                k = fills["pooled"] + gr
                bank_free(k)
                pe.matmul(ps[:, 6 + k % 2, 0:256], proj2[:, 0, P * gr:P * (gr + 1)], bands[:, gr, 0:256], start=True, stop=False)
                ins = pe.matmul(ps[:, 6 + k % 2, P:256], proj2[:, 1, P * gr:P * (gr + 1)], bands[:, gr, 256:384], start=False,
                                stop=True)
                ins.then_inc(t_ready[k % 2], 1)
            pe.wait_ge(odd_in, 32)
            for gr in range(4):
                k = fills["poolout"] + gr
                bank_free(k)
                pe.wait_ge(*emptied(fills["pooled"] + gr))
                pe.matmul(ps[:, 6 + k % 2, 0:256], pool_w[:, gr, :], pooledT[:, gr, :], start=True, stop=True).then_inc(
                    t_ready[k % 2], 1)
            pe.wait_ge(xn_done, 10)
            transposes("cq", lambda c, t: proj2[:, t, 512 + P * c:512 + P * (c + 1)], 3)
            transposes("ckv", lambda c, t: proj2[:, t, 896 + P * c:896 + P * (c + 1)], 2)
            for n, (name, parts, base) in enumerate((("uq", ((0, 512), (512, 768)), 0), ("ukv", ((0, 512), (512, 1024)), 3))):
                unit = units[groups[name][0]]
                if n == 0:
                    b = block_no[groups["in_odd"][2]]
                    pe.wait_ge(*taken[b])
                    pe.wait_ge(*taken[b - 1])
                    pe.wait_ge(*emptied(fills["cq"]))
                    pe.wait_ge(*emptied(fills["cq"] + 1))
                else:
                    pe.wait_ge(big_free, 1)
                    pe.wait_ge(*emptied(fills["ckv"]))
                for c in range(unit.quanta):
                    q = unit.first + c
                    pe.wait_ge(lo_done, q + 1)
                    for t in range(T):
                        for half, (a, b) in enumerate(parts):
                            ins = three(ps[:, 2 * t + half, 0:b - a], c_hi[:, base + c, P * t:P * (t + 1)],
                                        c_lo[:, base + c, P * t:P * (t + 1)], q % NQ, a, b, c == 0, c == unit.quanta - 1)
                    ins.then_inc(q_used, 1)
            pe.wait_ge(kf_done, 1)
            attention("d", qT2, kT2, D_QK, lambda m, t: qf[:, t, m, :], lambda m, t: kf[:, t, m, :])
            for qt in range(T):
                values(1, "d", e2, eT2, lambda m, kt: kv[:, kt, m, D_NOPE:2 * D_NOPE], D_V, qt)
            pe.wait_ge(o_free, 4)
            transposes("cat_odd", lambda c, t: proj2[:, t, P * c:P * (c + 1)], 4)
            pe.wait_ge(*emptied(fills["cat_odd"]))
            pe.wait_ge(*emptied(fills["cat_odd"] + 1))
            for b, u in enumerate(groups["out_odd"]):
                run_block(u, None)
            pe.wait_ge(xn_done, 12)
            transposes("router", lambda c, t: xn[:, t, P * c:P * (c + 1)], KC)
            k = fills["logits"]
            pe.wait_ge(*emptied(k - 1))
            bank_free(k)
            pe.wait_ge(rw_in, 16)
            for t in range(T):
                for c in range(KC):
                    ins = pe.matmul(ps[:, 6 + k % 2, NE * t:NE * (t + 1)], xT[:, c, P * t:P * (t + 1)], rw[:, c, :],
                                    start=(c == 0), stop=(c == KC - 1))
            ins.then_inc(t_ready[k % 2], 1)
            k = fills["prefix"]
            bank_free(k)
            pe.wait_ge(sel_done, 1)
            before, ones = con("before"), con("ones")
            o = ps[:, 6 + k % 2, :]
            pe.matmul(o[:, 0:NE], before, sel[:, 0, :], start=True, stop=True)
            pe.matmul(o[:, NE:2 * NE], before, sel[:, 1, :], start=True, stop=False)
            pe.matmul(o[:, NE:2 * NE], ones, sel[:, 0, :], start=False, stop=True)
            pe.matmul(o[:, 2 * NE:3 * NE], ones, sel[:, 0, :], start=True, stop=False)
            pe.matmul(o[:, 2 * NE:3 * NE], ones, sel[:, 1, :], start=False, stop=True).then_inc(t_ready[k % 2], 1)
            pe.wait_ge(routed, 1)
            pe.wait_ge(xn_rest, 2)
            with pe.Fori(0, ITEMS) as i:
                on = pe.value_load(active[0:1, bass.ds(i, 1)], min_val=0, max_val=1)
                with pe.If(on > 0):
                    def gate_up(kind, f):
                        part = 0 if kind == "gate" else 1
                        for kq in range(4):
                            q = 4 * pos_of[(kind, f)] + kq
                            pe.wait_ge(lo_done, Q1 + QI * i + q + 1)
                            for c in range(2):
                                kc = 2 * kq + c
                                ins = three(ps[:, 2 * (f % 2) + part, :], xg_hi[:, kc, :], xg_lo[:, kc, :], (Q1 + q) % NQ,
                                            512 * c, 512 * c + 512, kc == 0, kc == KC - 1)
                            ins.then_inc(q_used, 1)

                    def hidden(f):
                        pe.wait_ge(mul_done, FB * i + f + 1)
                        if f:
                            pe.wait_ge(hT_rest, FB * i + f)
                        for c in range(4):
                            ins = pe.transpose(ps[:, 7, P * c:P * (c + 1)], g_mul[:, P * c:P * (c + 1)], ident)
                        ins.then_inc(hT_ready, 1)

                    def down(f):
                        pe.wait_ge(hT_rest, FB * i + f + 1)
                        for c in range(4):
                            q = 4 * pos_of[("down", f)] + c
                            pe.wait_ge(lo_done, Q1 + QI * i + q + 1)
                            for half in range(2):
                                ins = three(ps[:, 4 + half, :], hT_hi[:, c, :], hT_lo[:, c, :], (Q1 + q) % NQ,
                                            512 * half, 512 * half + 512, f == 0 and c == 0, f == FB - 1 and c == 3)
                            ins.then_inc(q_used, 1)

                    pe.wait_ge(picked, i + 1)
                    for part, x in enumerate((xn_hi, xn_lo)):
                        for c in range(KC):
                            o = ps[:, 2 * part + c // 4, P * (c % 4):P * (c % 4 + 1)]
                            for t in range(T):
                                ins = pe.matmul(o, x[:, t, P * c:P * (c + 1)], pick[:, t, :], start=(t == 0), stop=(t == T - 1))
                    ins.then_inc(gathered, 1)
                    for t in range(T):
                        ins = pe.transpose(ps[:, 6, P * t:P * (t + 1)], pick[:, t, :].bitcast(F32), ident)
                    ins.then_inc(pickT_ready, 1)
                    pe.wait_ge(xg_head, i + 1)
                    pe.wait_ge(xg_rest, i + 1)
                    for f in range(FB):
                        if f >= 2:
                            pe.wait_ge(mul_done, FB * i + f - 1)
                        gate_up("gate", f)
                        if f:
                            hidden(f - 1)
                        gate_up("up", f)
                        if f:
                            down(f - 1)
                    hidden(FB - 1)
                    down(FB - 1)
                    pe.wait_ge(pickT_done, i + 1)
                    pe.wait_ge(y_rest, i + 1)
                    for t in range(T):
                        for half in range(2):
                            o = ps[:, 2 * t + half, :]
                            pe.matmul(o, pickT[:, P * t:P * (t + 1)], y_hi[:, 512 * half:512 * half + 512], start=True, stop=False)
                            ins = pe.matmul(o, pickT[:, P * t:P * (t + 1)], y_lo[:, 512 * half:512 * half + 512], start=False,
                                            stop=True)
                    ins.then_inc(scattered, 1)


INS = ["x", "norm_mix_even", "w_in_even", "lam_q1", "lam_k1", "lam_q2", "lam_k2", "subln_g", "sgu_ln_g", "sgu_ln_b",
       "sgu_w", "sgu_b", "w_out_even", "norm_ffn_even", "ffn_wg", "ffn_wu", "ffn_wd", "norm_mix_odd", "w_in_odd",
       "pool_w", "pool_scale", "q_norm_g", "w_uq", "kv_norm_g", "w_ukv", "w_out_odd", "norm_ffn_odd", "router",
       "moe_wg", "moe_wu", "moe_wd", "final_norm"]


def kernel(**inputs):
    import numpy as np
    import concourse.bacc as bacc
    from concourse.bass_utils import run_bass_kernel_spmd as run

    nc = bacc.Bacc("TRN2", target_bir_lowering=False, num_devices=1)
    arrays = {f"in_{n}": np.ascontiguousarray(inputs[n]) for n in INS}
    arrays["consts"], arrays["bands"] = constants()
    aps = {n: nc.dram_tensor(n, a.shape, mybir.dt.from_np(a.dtype), kind="ExternalInput").ap()
           for n, a in arrays.items()}
    out = nc.dram_tensor("out_0", (1, S, D), F32, kind="ExternalOutput").ap()
    trunk(nc, {n: aps[f"in_{n}"] for n in INS}, aps["consts"], aps["bands"], out)
    r = run(nc, [arrays], core_ids=[0])
    return r.results[0]["out_0"]
```

```python
import math
from contextlib import ExitStack

import numpy as np

import concourse.bass as bass
from concourse import mybir

F32 = mybir.dt.float32
F32R = mybir.dt.float32r
I32 = mybir.dt.int32
ALU = mybir.AluOpType
ACT = mybir.ActivationFunctionType
AX = mybir.AxisListType

P = 128
D = 1024
S = 256
T = S // P
KC = D // P
NORM_EPS = 1e-6
LN_EPS = 1e-5
MAPS = 8
A_HEADS, A_QK, A_HALF = 4, 64, 8
D_QK, D_NOPE, D_HALF, D_V = 96, 64, 16, 64
A_SCALE = A_QK ** -0.5
D_SCALE = D_QK ** -0.5
LAM_INIT = 0.8 - 0.6 * math.exp(0.0)
FFN = 2816
NE, FE = 8, 3584
FB = FE // 512
SLOTS = P
EXTRA = 2 * S // (SLOTS + 1)
ITEMS = NE + EXTRA
NEG = -1e30
CQ, CKV = 384, 256
WINDOWS = (2, 4, 8, 16)

CONST = {}
_at = 0
for _n, _w in (("ident", P), ("causal", P), ("iota", P), ("before", P), ("ones", P), ("ropeA", 2 * T * A_HALF),
               ("ropeD", 2 * T * D_HALF), ("lower8", NE * NE), ("iota8", NE)):
    CONST[_n] = (_at, _at + _w)
    _at += _w
CONSTS = _at


def constants():
    def rope(rot):
        f = np.float32
        inv = f(500000.0) ** (-np.arange(0, rot, 2, dtype=f) / f(rot))
        ang = np.arange(S, dtype=f)[:, None] * inv[None, :].astype(f)
        both = np.stack([np.cos(ang), np.sin(ang)])
        return both.reshape(2, T, P, rot // 2).transpose(2, 0, 1, 3).reshape(P, -1)
    i = np.arange(P)
    lower8 = (np.arange(NE)[None, :] < np.arange(NE)[:, None]).astype(np.float32).reshape(-1)
    parts = dict(ident=np.eye(P), causal=np.where(i[None, :] <= i[:, None], 0.0, NEG),
                 iota=np.tile(i, (P, 1)), before=(i[:, None] < i[None, :]), ones=np.ones((P, P)),
                 ropeA=rope(2 * A_HALF), ropeD=rope(2 * D_HALF),
                 lower8=np.tile(lower8, (P, 1)), iota8=np.tile(np.arange(NE), (P, 1)))
    table = np.concatenate([np.asarray(parts[n], np.float32) for n in CONST], axis=1)
    band = np.zeros((S, len(WINDOWS), S), np.float32)
    for g, w in enumerate(WINDOWS):
        for t in range(S):
            lo = max(t + 1 - w, 0)
            band[lo:t + 1, g, t] = np.float32(1.0) / np.float32(min(t + 1, w))
            band[t, g, t] -= 1.0
    bands = np.concatenate([band[:P], band[P:, :, P:]], axis=2)
    return table, np.ascontiguousarray(bands)


class Unit:
    def __init__(self, src, shape, quantum, first):
        self.src, self.shape, self.quantum = src, shape, quantum
        self.size = int(np.prod(shape))
        self.quanta = self.size // quantum
        self.first = first


def columns(w, c0, c1):
    return w[:, c0:c1].rearrange("(c p) n -> p c n", p=P)


def trunk(nc, A, consts_d, bands_d, out):
    units, groups = [], {}

    def add(name, src, shape, quantum):
        u = Unit(src, shape, quantum, units[-1].first + units[-1].quanta if units else 0)
        groups.setdefault(name, []).append(len(units))
        units.append(u)

    w_in_e, w_out_e = A["w_in_even"][0], A["w_out_even"][0]
    for b in (4, 3, 0, 1, 2):
        add("in_even", columns(w_in_e, 512 * b, 512 * b + 512), (KC, 512), 1024)
    for b in range(2):
        add("out_even", columns(w_out_e, 512 * b, 512 * b + 512), (KC, 512), 1024)
    widths = [min(512, FFN - f) for f in range(0, FFN, 512)]

    def add_down(f):
        w = widths[f]
        add("down", A["ffn_wd"][0][512 * f:512 * f + w, :].rearrange("(c p) n -> p c n", p=P), (w // P, D), 1024)

    for f, w in enumerate(widths):
        for name in ("wg", "wu"):
            add("gate" if name == "wg" else "up", columns(A["ffn_" + name][0], 512 * f, 512 * f + w), (KC, w), 1024)
        if f:
            add_down(f - 1)
    add_down(len(widths) - 1)
    w_in_o = A["w_in_odd"][0]
    for c0, c1 in ((0, 512), (512, 512 + CQ), (512 + CQ, 1184)):
        add("in_odd", columns(w_in_o, c0, c1), (KC, c1 - c0), 2 * (c1 - c0))
    add("uq", A["w_uq"][0].rearrange("(c p) n -> p c n", p=P), (3, 768), 768)
    add("ukv", A["w_ukv"][0].rearrange("(c p) n -> p c n", p=P), (2, 1024), 1024)
    for b in range(2):
        add("out_odd", columns(A["w_out_odd"][0], 512 * b, 512 * b + 512), (KC, 512), 1024)
    U1 = len(units)
    Q1 = units[-1].first + units[-1].quanta
    quanta = [(u, k) for u, unit in enumerate(units) for k in range(unit.quanta)]
    RING1, RING2, NQ = 4, 7, 4
    ORDER = []
    for f in range(FB):
        ORDER += [("gate", f), ("up", f)]
        if f:
            ORDER.append(("down", f - 1))
    ORDER.append(("down", FB - 1))
    UI = len(ORDER)
    QI = 4 * UI
    EARLY = 2
    AHEAD = NQ + 1
    assert UI % RING2 == 0 and QI % NQ == 0 and U1 % RING1 == 0
    pos_of = {o: n for n, o in enumerate(ORDER)}

    fills, n = {}, 0
    for name, k in (("mix_even", 4), ("sgu_w", 1), ("mixed", 2), ("qk_a", 8), ("pT_a", 6), ("cat_even", 4), ("ffn", 4),
                    ("mix_odd", 4), ("pooled", 4), ("poolout", 4), ("cq", 2), ("ckv", 1), ("qk_d", 8), ("pT_d", 6),
                    ("cat_odd", 2), ("router", 4), ("logits", 1), ("prefix", 1)):
        fills[name] = n
        n += k

    fills["pT_a1"], fills["pT_d1"] = fills["pT_a"] + 2, fills["pT_d"] + 2

    with ExitStack() as ctx:
        def sbuf(name, shape, dt=F32, on=ctx):
            return on.enter_context(nc.sbuf_tensor(name, [P] + list(shape), dt))

        def sem(name):
            return ctx.enter_context(nc.semaphore(name))

        ring_a = sbuf("ring_a", [RING1, 4096])
        w_hi = sbuf("w_hi", [NQ, 1024], F32R)
        w_lo = sbuf("w_lo", [NQ, 1024], F32R)
        h = sbuf("h", [T, D])
        table = sbuf("table", [CONSTS])
        stats = sbuf("stats", [96])
        slot_of = sbuf("slot_of", [T, ITEMS + 1])
        gate_of = sbuf("gate_of", [T, ITEMS])
        active = ctx.enter_context(nc.sbuf_tensor("active", [1, ITEMS + 1], I32))
        expert = ctx.enter_context(nc.sbuf_tensor("expert", [1, ITEMS], I32))
        xn = sbuf("xn", [T, D])
        xt_hi = sbuf("xt_hi", [KC, S], F32R)
        xt_lo = sbuf("xt_lo", [KC, S], F32R)
        gain = sbuf("gain", [D])

        even = ExitStack()
        proj = sbuf("proj", [T, 2560], on=even)
        qT = sbuf("qT", [MAPS, S], on=even)
        kT = sbuf("kT", [MAPS, S], on=even)
        e = sbuf("e", [MAPS, S], on=even)
        eT = sbuf("eT", [T, MAPS, P], on=even)
        sgu_w = sbuf("sgu_w_sb", [4, P], on=even)
        sgu_wT = sbuf("sgu_wT", [4, P], on=even)
        sgu_b = sbuf("sgu_b_sb", [4], on=even)
        subln = sbuf("subln", [P], on=even)
        lamv = sbuf("lamv", [4, 64], on=even)
        lamj = sbuf("lamj", [2, 64], on=even)
        even.close()
        dense = ExitStack()
        f_hi = sbuf("f_hi", [2, 4, S], F32R, on=dense)
        f_lo = sbuf("f_lo", [2, 4, S], F32R, on=dense)
        dense.close()
        odd = ExitStack()
        proj2 = sbuf("proj2", [T, 1184], on=odd)
        qT2 = sbuf("qT2", [MAPS, S], on=odd)
        kT2 = sbuf("kT2", [MAPS, S], on=odd)
        e2 = sbuf("e2", [MAPS, S], on=odd)
        eT2 = sbuf("eT2", [T, MAPS, P], on=odd)
        qf = sbuf("qf", [T, MAPS, D_QK], on=odd)
        kv = sbuf("kv", [T, MAPS, 2 * D_NOPE], on=odd)
        pool_w = sbuf("pool_w_sb", [4, P], on=odd)
        pool_s = sbuf("pool_s", [4], on=odd)
        c_hi = sbuf("c_hi", [5, S], F32R, on=odd)
        c_lo = sbuf("c_lo", [5, S], F32R, on=odd)
        odd.close()
        route = ExitStack()
        xT = sbuf("xT", [KC, S], on=route)
        rw = sbuf("rw", [KC, NE], on=route)
        lg = sbuf("lg", [T, NE], on=route)
        top = sbuf("top", [T, 8], on=route)
        cmp1 = sbuf("cmp1", [T, NE, NE], on=route)
        cmp2 = sbuf("cmp2", [T, NE, NE], on=route)
        rank = sbuf("rank", [T, NE], on=route)
        sel = sbuf("sel", [T, NE], on=route)
        gate = sbuf("gate", [T, NE], on=route)
        gtmp = sbuf("gtmp", [T, NE], on=route)
        place = sbuf("place", [T, NE], on=route)
        over = sbuf("over", [4, NE], on=route)
        wts = sbuf("wts", [T, 4], on=route)
        route.close()
        xg_hi = sbuf("xg_hi", [KC, P], F32R)
        xg_lo = sbuf("xg_lo", [KC, P], F32R)
        hT_hi = sbuf("hT_hi", [4, P], F32R)
        hT_lo = sbuf("hT_lo", [4, P], F32R)
        y_hi = sbuf("y_hi", [D], F32R)
        y_lo = sbuf("y_lo", [D], F32R)
        pick = sbuf("pick", [T, SLOTS], F32R)
        pickT = sbuf("pickT", [S], F32R)
        ring_b = sbuf("ring_b", [RING2 - RING1, 4096])
        g_act = xn[:, 0, 0:512]
        g_mul = xn[:, 0, 512:1024]
        xn_hi = xt_hi[:, :, :].rearrange("p c s -> p (c s)").rearrange("p (t d) -> p t d", t=T)
        xn_lo = xt_lo[:, :, :].rearrange("p c s -> p (c s)").rearrange("p (t d) -> p t d", t=T)
        e_first = xn[:, 0, :].rearrange("p (m k) -> p m k", m=MAPS)
        kf = xn[:, :, 0:768].rearrange("p t (m d) -> p t m d", m=MAPS)
        bands = eT2[:, :, :, :].rearrange("p t m q -> p (t m q)")[:, 0:4 * 384].rearrange("p (g s) -> p g s", g=4)
        pooledT = e2[:, 0:4, :]

        ps = ctx.enter_context(nc.psum_tensor("ps", [P, 8, 512], F32))
        flat = ps[:, :, :].rearrange("p b n -> p (b n)")

        def st(name, k=0, n=None):
            at, w = dict(SSQ=(0, 8), MS=(8, 8), ROOT=(16, 8), NEGMAX=(24, 8), ESUM=(32, 8), MAX=(40, 8), EINV=(48, 8),
                         SUM=(56, 2), NEGMU=(58, 2), VSQ=(60, 2), LDOT=(62, 2), LEXP=(64, 2), NLAM=(66, 1), TMP=(67, 1),
                         JUNK=(68, 1), MARK=(69, 1), LEFT=(70, 1), NEGMAX1=(72, 8), ESUM1=(80, 8),
                         EINV1=(88, 8))[name]
            return stats[:, at + k:at + k + (w if n is None else n)]

        def con(name):
            a, b = CONST[name]
            return table[:, a:b]
        ident = con("ident")

        def slot(s):
            return ring_a[:, s] if s < RING1 else ring_b[:, s - RING1]

        const_in, x_in, gain_in, even_in, bands_in, odd_in, rw_in = map(sem, (
            "const_in", "x_in", "gain_in", "even_in", "bands_in", "odd_in", "rw_in"))
        loaded = [sem(f"loaded{s}") for s in range(RING2)]
        hi_done, lo_done, q_used = sem("hi_done"), sem("lo_done"), sem("q_used")
        t_ready = [sem("t_ready0"), sem("t_ready1")]
        t_free = [sem("t_free0"), sem("t_free1")]
        t_head = sem("t_head")
        blk_free = [sem("blk_free0"), sem("blk_free1")]
        ssq_done, ms_done, root_done, xn_begun, xn_done = map(sem, (
            "ssq_done", "ms_done", "root_done", "xn_begun", "xn_done"))
        act_chain, dve_chain = sem("act_chain"), sem("dve_chain")
        roped, lam_dot, lam_exp = sem("roped"), sem("lam_dot"), sem("lam_exp")
        mu_done, vsq_done, ln_applied, oa_done = map(sem, ("mu_done", "vsq_done", "ln_applied", "oa_done"))
        sgu_masked = sem("sgu_masked")
        scored, negmax, exped, o_ready, o_free = map(sem, ("scored", "negmax", "exped", "o_ready", "o_free"))
        fsilu, fmul, f_head, f_done, down_added = map(sem, ("fsilu", "fmul", "f_head", "f_done", "down_added"))
        kf_done, big_free = sem("kf_done"), sem("big_free")
        h_done = sem("h_done")
        top_done, top_exp, sel_done, routed, xn_head, xn_rest = map(sem, ("top_done", "top_exp", "sel_done", "routed", "xn_head", "xn_rest"))
        picked, gathered, pickT_ready, pickT_done, xg_head, xg_rest = map(sem, (
            "picked", "gathered", "pickT_ready", "pickT_done", "xg_head", "xg_rest"))
        silu_done, mul_done, hT_ready, hT_head, hT_rest = map(sem, (
            "silu_done", "mul_done", "hT_ready", "hT_head", "hT_rest"))
        y_head, y_rest, scattered, added = map(sem, ("y_head", "y_rest", "scattered", "added"))
        experts_done, out_ready, stored = sem("experts_done"), sem("out_ready"), sem("stored")

        block = ctx.enter_context(nc.Block())

        def filled(k):
            return t_ready[k % 2], k // 2 + 1

        def emptied(k):
            return t_free[k % 2], k // 2 + 1

        blocks = [u for name in ("in_even", "out_even", "in_odd", "out_odd") for u in groups[name]]
        block_no = {u: n for n, u in enumerate(blocks)}

        taken, seen = [], [0, 0, 0]
        for n, u in enumerate(blocks):
            if u in groups["out_even"] + groups["out_odd"]:
                seen[2] += 1
                taken.append((h_done, seen[2]))
            else:
                seen[n % 2] += 1
                taken.append((blk_free[n % 2], seen[n % 2]))

        def used(u):
            return q_used, units[u].first + units[u].quanta

        def block_banks(n):
            return 2 * (n % 2)

        @block.sync
        def _(sp):
            sp.dma_start(h[:, :, :], A["x"][0].rearrange("(t p) d -> p t d", p=P)).then_inc(x_in, 16)
            sp.dma_start(table[:, :], consts_d).then_inc(const_in, 16)
            for u, unit in enumerate(units):
                if u >= RING1:
                    before = units[u - RING1]
                    sp.wait_ge(lo_done, before.first + before.quanta)
                sp.dma_start(slot(u % RING1)[:, 0:unit.size].rearrange("p (c n) -> p c n", c=unit.shape[0]),
                             unit.src).then_inc(loaded[u % RING1], 16)

            def source(kind, f, ex):
                if kind == "down":
                    return A["moe_wd"][0][ex][512 * f:512 * f + 512, :].rearrange("(c p) n -> p c n", p=P)
                return A["moe_wg" if kind == "gate" else "moe_wu"][0][ex][:, 512 * f:512 * f + 512].rearrange(
                    "(c p) n -> p c n", p=P)

            def load(j, i, ex, wait=True):
                kind, f = ORDER[j]
                if wait:
                    sp.wait_ge(lo_done, Q1 + QI * i + 4 * (j - RING2 + 1))
                c = 4 if kind == "down" else KC
                sp.dma_start(slot(j % RING2).rearrange("p (c n) -> p c n", c=c), source(kind, f, ex)).then_inc(
                    loaded[j % RING2], 16)

            for j in range(RING2):
                if j < RING1:
                    last = units[U1 - RING1 + j]
                    sp.wait_ge(lo_done, last.first + last.quanta)
                elif j == RING1:
                    sp.wait_ge(h_done, 4)
                load(j, 0, 0, wait=False)
            for j in range(RING2, UI):
                load(j, 0, 0)
            with sp.Fori(1, NE) as i:
                for j in range(UI):
                    load(j, i, i)
            sp.wait_ge(routed, 1)
            with sp.Fori(NE, ITEMS) as i:
                on = sp.value_load(active[0:1, bass.ds(i, 1)], min_val=0, max_val=1)
                with sp.If(on > 0):
                    ex = sp.value_load(expert[0:1, bass.ds(i, 1)], min_val=0, max_val=NE - 1)
                    for j in range(UI):
                        load(j, i, ex)
            for t in range(T):
                sp.wait_ge(out_ready, t + 1)
                sp.dma_start(out[0].rearrange("(t p) d -> p t d", p=P)[:, t], xn[:, t, :]).then_inc(stored, 16)
            sp.wait_ge(stored, 16 * T)

        @block.gpsimd
        def _(pool):
            def gains(*parts):
                at = 0
                for v, w in parts:
                    pool.dma_start(gain[:, at:at + w], v.partition_broadcast(P)).then_inc(gain_in, 16)
                    at += w
            gains((A["norm_mix_even"][0], D))
            for n, v in enumerate(("lam_q1", "lam_k1", "lam_q2", "lam_k2")):
                pool.dma_start(lamv[:, n, :], A[v][0].partition_broadcast(P)).then_inc(even_in, 16)
            pool.dma_start(sgu_w[:, :, :], A["sgu_w"][0].rearrange("g p q -> p g q")).then_inc(even_in, 16)
            with nc.allow_non_contiguous_dma("512 words, once"):
                pool.dma_start(sgu_b[:, :], A["sgu_b"][0].rearrange("g p -> p g")).then_inc(even_in, 16)
            pool.dma_start(subln[:, :], A["subln_g"][0].partition_broadcast(P)).then_inc(even_in, 16)
            pool.wait_ge(xn_done, 2)
            gains((A["sgu_ln_g"][0], 512), (A["sgu_ln_b"][0], 512))
            pool.wait_ge(even_in, 16 * 7)
            pool.affine_select(out=sgu_w[:, :, :], in_=sgu_w[:, :, :], compare_op=ALU.is_ge, fill=0.0, base=0,
                               pattern=[[0, 4], [-1, P]], channel_multiplier=1).then_inc(sgu_masked, 1)
            pool.wait_ge(ln_applied, 2)
            gains((A["norm_ffn_even"][0], D))
            pool.wait_ge(xn_done, 4)
            gains((A["norm_mix_odd"][0], D))
            pool.wait_ge(down_added, 2)
            pool.dma_start(bands, bands_d).then_inc(bands_in, 16)
            pool.dma_start(pool_w[:, :, :], A["pool_w"][0].rearrange("g c d -> c g d")).then_inc(odd_in, 16)
            with nc.allow_non_contiguous_dma("512 words, once"):
                pool.dma_start(pool_s[:, :], A["pool_scale"][0].rearrange("(g d) -> d g", d=P)).then_inc(odd_in, 16)
            pool.wait_ge(xn_done, 6)
            gains((A["q_norm_g"][0], CQ), (A["kv_norm_g"][0], CKV))
            pool.wait_ge(xn_done, 10)
            gains((A["norm_ffn_odd"][0], D))
            pool.wait_ge(h_done, 4)
            pool.dma_start(rw[:, :, :], A["router"][0].rearrange("(c p) n -> p c n", p=P)).then_inc(rw_in, 16)
            pool.wait_ge(xn_done, 12)
            gains((A["final_norm"], D))

        @block.scalar
        def _(act):
            chain = [0]
            split = [0]

            def link(ins):
                chain[0] += 1
                ins.then_inc(act_chain, 1)
                act.wait_ge(act_chain, chain[0])

            def hi_upto(n):
                while split[0] < min(n, Q1):
                    q = split[0]
                    u, k = quanta[q]
                    w = units[u].quantum
                    if k == 0:
                        act.wait_ge(loaded[u % RING1], 16 * (u // RING1 + 1))
                    if q >= NQ:
                        act.wait_ge(q_used, q - NQ + 1)
                    nc.scalar.activation(w_hi[:, q % NQ, 0:w], slot(u % RING1)[:, k * w:(k + 1) * w],
                                         ACT.Copy).then_inc(hi_done, 1)
                    split[0] += 1

            def ahead(u):
                hi_upto(units[u].first + units[u].quanta + NQ - 1)

            def norm_sums(srcs, junk):
                for c, src in enumerate(srcs):
                    nc.scalar.activation(junk[c], src, ACT.Square, accum_out=st("SSQ", c, 1)).then_inc(ssq_done, 1)

            def half_sums(half, done):
                act.wait_ge(h_done, done)
                for t in range(T):
                    cols = slice(512 * half, 512 * half + 512)
                    nc.scalar.activation(xn[:, t, cols], h[:, t, cols], ACT.Square,
                                         accum_out=st("SSQ", 2 * half + t, 1)).then_inc(ssq_done, 1)

            def root(n, w):
                act.wait_ge(ms_done, n)
                nc.scalar.activation(st("ROOT", 0, w), st("MS", 0, w), ACT.Sqrt).then_inc(root_done, 1)

            def heads(name, dst, count=4, chunks=2, base=0, start=0):
                for f in range(start, count):
                    k = fills[name] + f
                    act.wait_ge(*filled(k))
                    n = min(chunks, dst[1] - 2 * f)
                    nc.scalar.activation(dst[0][:, base + 2 * f:base + 2 * f + n, :],
                                         flat[:, 512 * (6 + k % 2):512 * (6 + k % 2) + 256 * n].rearrange(
                                             "p (c s) -> p c s", c=n), ACT.Copy).then_inc(t_head, 1)

            def block_psum(n, w):
                b = block_banks(n)
                return ps[:, b:b + 2, 0:w]

            def copy_block(u, dst, w, func=ACT.Copy):
                n = block_no[u]
                act.wait_ge(*used(u))
                return nc.scalar.activation(dst, block_psum(n, w), func).then_inc(blk_free[n % 2], 1)

            act.wait_ge(x_in, 16)
            norm_sums([h[:, t, :] for t in range(T)], [xn[:, t, :] for t in range(T)])
            root(1, 2)
            heads("mix_even", (xt_hi, KC), count=2)
            hi_upto(2)
            heads("mix_even", (xt_hi, KC), start=2)
            hi_upto(NQ)
            g = groups["in_even"]
            ahead(g[0])
            act.wait_ge(*used(g[0]))
            for t in range(T):
                last = nc.scalar.activation(proj[:, t, 2048:2560], ps[:, block_banks(0) + t, :], ACT.Gelu_apprx_tanh,
                                            accum_out=st("SUM", t, 1))
            last.then_inc(blk_free[0], 1)
            ahead(g[1])
            copy_block(g[1], proj[:, :, 1536:2048], 512, ACT.Gelu_apprx_tanh)
            for t in range(T):
                if t == 0:
                    act.wait_ge(mu_done, 1)
                nc.scalar.activation(e[:, 2 * t:2 * t + 2, :], proj[:, t, 2048:2560].rearrange("p (a s) -> p a s", a=2),
                                     ACT.Square, bias=st("NEGMU", t, 1),
                                     accum_out=st("VSQ", t, 1)).then_inc(vsq_done, 1)
            root(2, 2)
            for b in range(2):
                ahead(g[2 + b])
                copy_block(g[2 + b], proj[:, :, 512 * b:512 * b + 512], 512)

            def evac_half(name, dst, count, parity):
                for f in range(count):
                    k = fills[name] + f
                    if k % 2 == parity:
                        act.wait_ge(*filled(k))
                        nc.scalar.activation(*dst(f, k), ACT.Copy).then_inc(t_free[k % 2], 1)

            def qk_fill(qt_, kt_, w):
                def at(f, k):
                    to = qt_ if f < 4 else kt_
                    m = 2 * (f % 4)
                    return (to[0:w, m:m + 2, :],
                            ps[0:w, 6 + k % 2, :].rearrange("p (m s) -> p m s", m=2))
                return at

            def pT_fill(et, qt):
                def at(f, k):
                    if qt == 0:
                        kt, m = 0, 4 * f
                    else:
                        kt, m = f // 2, 4 * (f % 2)
                    return et[:, kt, m:m + 4, :], ps[:, 6 + k % 2, :].rearrange("p (m s) -> p m s", m=4)
                return at

            def exponentials(L, ee, qt):
                act.wait_ge(negmax, 2 * L + qt + 1)
                mine, neg, total = ((e_first, "NEGMAX", "ESUM"), (ee, "NEGMAX1", "ESUM1"))[qt]
                w = P * (qt + 1)
                for m in range(MAPS):
                    ins = nc.scalar.activation(mine[:, m, 0:w], mine[:, m, 0:w], ACT.Exp, bias=st(neg, m, 1),
                                               accum_out=st(total, m, 1))
                ins.then_inc(exped, 1)

            k = fills["sgu_w"]
            act.wait_ge(*filled(k))
            nc.scalar.activation(sgu_wT[:, :, :], ps[:, 6 + k % 2, :].rearrange("p (g q) -> p g q", g=4),
                                 ACT.Copy).then_inc(t_free[k % 2], 1)
            evac_half("qk_a", qk_fill(qT, kT, A_QK), 8, 0)
            act.wait_ge(lam_dot, 1)
            nc.scalar.activation(st("LEXP"), st("LDOT"), ACT.Exp).then_inc(lam_exp, 1)
            exponentials(0, e, 0)
            ahead(g[4])
            copy_block(g[4], proj[:, :, 1024:1536], 512)
            evac_half("pT_a", pT_fill(eT, 0), 2, 0)
            exponentials(0, e, 1)
            evac_half("pT_a1", pT_fill(eT, 1), 4, 0)
            root(3, 8)
            heads("cat_even", (xt_hi, KC))
            for b, u in enumerate(groups["out_even"]):
                ahead(u)
                half_sums(b, b + 1)
            root(4, 2)
            heads("ffn", (xt_hi, KC))
            for f, w in enumerate(widths):
                c = w // P
                ahead(groups["up"][f])
                act.wait_ge(*used(groups["up"][f]))
                silu_to = xn[:, 0, :].rearrange("p (c s) -> p c s", c=4)[:, 0:c, :]
                if f:
                    act.wait_ge(f_done, f)
                nc.scalar.activation(silu_to, ps[:, 0:c, 0:256], ACT.Silu).then_inc(fsilu, 1)
                act.wait_ge(fmul, f + 1)
                nc.scalar.activation(f_hi[:, f % 2, 0:c, :], silu_to, ACT.Copy).then_inc(f_head, 1)
            ahead(groups["down"][-1])
            act.wait_ge(down_added, 2)
            norm_sums([h[:, t, :] for t in range(T)], [xn[:, t, :] for t in range(T)])
            root(5, 2)
            heads("mix_odd", (xt_hi, KC))
            for u, (c0, c1) in zip(groups["in_odd"], ((0, 512), (512, 512 + CQ), (512 + CQ, 1184))):
                ahead(u)
                copy_block(u, proj2[:, :, c0:c1], c1 - c0)
            n = block_no[groups["in_odd"][2]]
            act.wait_ge(*taken[n])
            act.wait_ge(*taken[n - 1])
            norm_sums([proj2[:, t, 512:512 + CQ] for t in range(T)] + [proj2[:, t, 896:896 + CKV] for t in range(T)],
                      [xn[:, t, 0:CQ] for t in range(T)] + [xn[:, t, 512:512 + CKV] for t in range(T)])
            root(6, 4)
            for f in range(4):
                k = fills["pooled"] + f
                act.wait_ge(*filled(k))
                nc.scalar.activation(pooledT[:, f, :], ps[:, 6 + k % 2, 0:256], ACT.Copy).then_inc(t_free[k % 2], 1)
            for f in range(4):
                k = fills["poolout"] + f
                act.wait_ge(*filled(k))
                if f == 0:
                    act.wait_ge(odd_in, 32)
                nc.scalar.activation(xt_hi[:, f, :], ps[:, 6 + k % 2, 0:256], ACT.Copy,
                                     scale=pool_s[:, f:f + 1]).then_inc(t_head, 1)
            heads("cq", (c_hi, 3), count=2)
            heads("ckv", (c_hi, 2), count=1, base=3)
            for n, u in enumerate((groups["uq"][0], groups["ukv"][0])):
                ahead(u)
                act.wait_ge(*used(u))
                for t in range(T):
                    if n == 0:
                        ins = nc.scalar.activation(qf[:, t, :, :].rearrange("p m d -> p (m d)"),
                                                   flat[:, 1024 * t:1024 * t + 768], ACT.Copy)
                    else:
                        ins = nc.scalar.activation(kv[:, t, :, :].rearrange("p m d -> p (m d)"),
                                                   flat[:, 1024 * t:1024 * t + 1024], ACT.Copy)
                ins.then_inc(big_free, 1)
            evac_half("qk_d", qk_fill(qT2, kT2, D_QK), 8, 0)
            exponentials(1, e2, 0)
            evac_half("pT_d", pT_fill(eT2, 0), 2, 0)
            exponentials(1, e2, 1)
            evac_half("pT_d1", pT_fill(eT2, 1), 4, 0)
            heads("cat_odd", (xt_hi, 8), count=2, base=4)
            for b, u in enumerate(groups["out_odd"]):
                ahead(u)
                half_sums(b, b + 3)
            root(7, 2)
            for f in range(4):
                k = fills["router"] + f
                if k % 2 == 0:
                    act.wait_ge(*filled(k))
                    nc.scalar.activation(xT[:, 2 * f:2 * f + 2, :], ps[:, 6 + k % 2, :].rearrange("p (c s) -> p c s", c=2),
                                         ACT.Copy).then_inc(t_free[k % 2], 1)
            act.wait_ge(xn_done, 12)
            for t in range(T):
                nc.scalar.activation(xn_hi[:, t, :], xn[:, t, :], ACT.Copy).then_inc(xn_head, 1)
            act.wait_ge(top_done, 1)
            nc.scalar.activation(wts[:, :, 1:2], wts[:, :, 0:1], ACT.Exp).then_inc(top_exp, 1)
            assert split[0] == Q1

            def expert_head(i, q):
                j, k = q // 4, q % 4
                if k == 0:
                    fills_before = U1 // RING1 if j % RING2 < RING1 else 0
                    act.wait_ge(loaded[j % RING2], 16 * (fills_before + UI // RING2 * i + j // RING2 + 1))
                act.wait_ge(q_used, Q1 + QI * i + q - NQ + 1)
                nc.scalar.activation(w_hi[:, (Q1 + q) % NQ, :], slot(j % RING2)[:, 1024 * k:1024 * k + 1024],
                                     ACT.Copy).then_inc(hi_done, 1)

            def gathered_heads(n):
                act.wait_ge(gathered, n + 1)
                nc.scalar.activation(xg_hi[:, :, :], ps[:, 0:2, :].rearrange("p b (c s) -> p (b c) s", s=P),
                                     ACT.Copy).then_inc(xg_head, 1)

            for q in range(NQ - 1):
                expert_head(0, q)
            gathered_heads(0)
            for q in range(NQ - 1, AHEAD):
                expert_head(0, q)
            act.wait_ge(routed, 1)
            with act.Fori(0, ITEMS) as i:
                on = act.value_load(active[0:1, bass.ds(i, 1)], min_val=0, max_val=1)
                with act.If(on > 0):
                    done = [AHEAD]

                    def heads_upto(n):
                        while done[0] < min(n, QI):
                            expert_head(i, done[0])
                            done[0] += 1

                    def heads_ahead(unit):
                        heads_upto(4 * (pos_of[unit] + 1) + NQ - 1)

                    def hT_heads(f):
                        act.wait_ge(hT_ready, FB * i + f + 1)
                        nc.scalar.activation(hT_hi[:, :, :], ps[:, 7, :].rearrange("p (c s) -> p c s", c=4),
                                             ACT.Copy).then_inc(hT_head, 1)

                    heads_upto(NQ + EARLY)
                    act.wait_ge(q_used, Q1 + QI * i + EARLY + 1)
                    act.wait_ge(pickT_ready, i + 1)
                    nc.scalar.activation(pickT[:, :], ps[:, 6, 0:S], ACT.Copy).then_inc(pickT_done, 1)
                    for f in range(FB):
                        if f:
                            heads_ahead(("gate", f))
                            hT_heads(f - 1)
                        heads_ahead(("up", f))
                        act.wait_ge(q_used, Q1 + QI * i + 4 * (pos_of[("up", f)] + 1))
                        if f:
                            act.wait_ge(mul_done, FB * i + f)
                        nc.scalar.activation(g_act, ps[:, 2 * (f % 2), :], ACT.Silu).then_inc(silu_done, 1)
                    heads_ahead(("down", FB - 2))
                    hT_heads(FB - 1)
                    gathered_heads(i + 1)
                    heads_upto(QI)
                    following = act.value_load(active[0:1, bass.ds(i + 1, 1)], min_val=0, max_val=1)
                    with act.If(following > 0):
                        for q in range(NQ - 1):
                            expert_head(i, QI + q)
                    act.wait_ge(q_used, Q1 + QI * (i + 1))
                    for half in range(2):
                        nc.scalar.activation(y_hi[:, 512 * half:512 * half + 512], ps[:, 4 + half, :],
                                             ACT.Copy).then_inc(y_head, 1)
                    with act.If(following > 0):
                        for q in range(NQ - 1, AHEAD):
                            expert_head(i, QI + q)
            act.wait_ge(experts_done, 1)
            norm_sums([h[:, t, :] for t in range(T)], [xn[:, t, :] for t in range(T)])
            root(8, 2)

        @block.vector
        def _(dve):
            chain = [0]
            split = [0]
            v = nc.vector

            def link(ins):
                chain[0] += 1
                ins.then_inc(dve_chain, 1)
                dve.wait_ge(dve_chain, chain[0])

            def lo_upto(n):
                while split[0] < min(n, Q1):
                    q = split[0]
                    u, k = quanta[q]
                    w = units[u].quantum
                    dve.wait_ge(hi_done, q + 1)
                    v.tensor_tensor(w_lo[:, q % NQ, 0:w], slot(u % RING1)[:, k * w:(k + 1) * w],
                                    w_hi[:, q % NQ, 0:w].bitcast(F32), ALU.subtract).then_inc(lo_done, 1)
                    split[0] += 1

            def ahead(u):
                lo_upto(units[u].first + units[u].quanta + NQ - 1)

            ssq = [0]
            gains = [0]

            def mean_eps(w, width, eps=NORM_EPS, src="SSQ"):
                v.tensor_scalar(st("MS", 0, w), st(src, 0, w), 1.0 / width, eps, ALU.mult, ALU.add).then_inc(ms_done, 1)

            def inverse(n, w):
                dve.wait_ge(root_done, n)
                link(v.reciprocal(st("ROOT", 0, w), st("ROOT", 0, w)))

            def rmsnorm(n, gain_count, halves=False):
                ssq[0] += 4 if halves else 2
                dve.wait_ge(ssq_done, ssq[0])
                if halves:
                    link(v.tensor_tensor(st("SSQ", 0, 2), st("SSQ", 0, 2), st("SSQ", 2, 2), ALU.add))
                mean_eps(2, D)
                inverse(n, 2)
                dve.wait_ge(gain_in, 16 * gain_count)
                for half in range(2):
                    cols = slice(512 * half, 512 * half + 512)
                    for t in range(T):
                        v.scalar_tensor_tensor(out=xn[:, t, cols], in0=h[:, t, cols], scalar=st("ROOT", t, 1),
                                               in1=gain[:, cols], op0=ALU.mult, op1=ALU.mult).then_inc(
                                                   xn_done if half else xn_begun, 1)

            heads_seen = [0]

            def rests(name, dst, count=4, base=0, start=0):
                for f in range(start, count):
                    k = fills[name] + f
                    n = min(2, dst[2] - 2 * f)
                    heads_seen[0] += 1
                    dve.wait_ge(t_head, heads_seen[0])
                    v.tensor_tensor(dst[1][:, base + 2 * f:base + 2 * f + n, :],
                                    flat[:, 512 * (6 + k % 2):512 * (6 + k % 2) + 256 * n].rearrange(
                                        "p (c s) -> p c s", c=n),
                                    dst[0][:, base + 2 * f:base + 2 * f + n, :].bitcast(F32),
                                    ALU.subtract).then_inc(t_free[k % 2], 1)

            def rope(x, tab, half, G, tmp):
                a, _ = CONST[tab]
                cs = [table[:, a + n * T * half:a + (n + 1) * T * half].rearrange("p (t u k) -> p t u k", t=T, u=1)
                      .to_broadcast([P, T, G, half]) for n in range(2)]
                x1, x2 = x[:, :, :, 0:half], x[:, :, :, half:2 * half]
                v.tensor_tensor(tmp[0], x1, cs[0], ALU.mult)
                v.tensor_tensor(tmp[1], x2, cs[1], ALU.mult)
                v.tensor_tensor(tmp[2], x2, cs[0], ALU.mult)
                link(v.tensor_tensor(tmp[3], x1, cs[1], ALU.mult))
                v.tensor_tensor(x1, tmp[0], tmp[1], ALU.subtract)
                return v.tensor_tensor(x2, tmp[2], tmp[3], ALU.add)

            def scratch(buf, G, half):
                f = buf[:, :, :].rearrange("p m s -> p (m s)")
                w = T * G * half
                return [f[:, n * w:(n + 1) * w].rearrange("p (t g k) -> p t g k", t=T, g=G) for n in range(4)]

            def evac_half(name, dst, count, parity):
                for f in range(count):
                    k = fills[name] + f
                    if k % 2 == parity:
                        dve.wait_ge(*filled(k))
                        v.tensor_copy(*dst(f, k)).then_inc(t_free[k % 2], 1)

            def qk_fill(qt_, kt_, w):
                def at(f, k):
                    to = qt_ if f < 4 else kt_
                    m = 2 * (f % 4)
                    return (to[0:w, m:m + 2, :],
                            ps[0:w, 6 + k % 2, :].rearrange("p (m s) -> p m s", m=2))
                return at

            def pT_fill(et, qt):
                def at(f, k):
                    if qt == 0:
                        kt, m = 0, 4 * f
                    else:
                        kt, m = f // 2, 4 * (f % 2)
                    return et[:, kt, m:m + 4, :], ps[:, 6 + k % 2, :].rearrange("p (m s) -> p m s", m=4)
                return at

            causal = con("causal").rearrange("p (u k) -> p u k", u=1).to_broadcast([P, MAPS, P])

            def scores(L, ee, scale, qt):
                dve.wait_ge(scored, 2 * L + qt + 1)
                mine, neg = ((e_first, "NEGMAX"), (ee, "NEGMAX1"))[qt]
                if qt == 0:
                    link(v.scalar_tensor_tensor(out=mine, in0=ps[:, 4:6, :].rearrange("p b (m k) -> p (b m) k", k=P),
                                                scalar=scale, in1=causal, op0=ALU.mult, op1=ALU.add))
                else:
                    sc = ps[:, 0:4, :].rearrange("p b (m k) -> p (b m) k", k=S)
                    v.tensor_scalar(mine[:, :, 0:P], sc[:, :, 0:P], scale, None, ALU.mult)
                    link(v.scalar_tensor_tensor(out=mine[:, :, P:S], in0=sc[:, :, P:S], scalar=scale, in1=causal,
                                                op0=ALU.mult, op1=ALU.add))
                link(v.reduce_max(st("MAX"), mine[:, :, 0:P * (qt + 1)], AX.X))
                v.tensor_scalar(st(neg), st("MAX"), -1.0, None, ALU.mult).then_inc(negmax, 1)

            def sums(L, qt):
                dve.wait_ge(exped, 2 * L + qt + 1)
                link(v.reciprocal(st(("EINV", "EINV1")[qt]), st(("ESUM", "ESUM1")[qt])))

            dve.wait_ge(const_in, 16)
            rmsnorm(1, 1)
            rests("mix_even", (xt_hi, xt_lo, KC), count=2)
            lo_upto(2)
            rests("mix_even", (xt_hi, xt_lo, KC), start=2)
            lo_upto(NQ)
            g = groups["in_even"]
            ahead(g[0])
            dve.wait_ge(even_in, 16 * 7)
            for n in range(2):
                ins = v.tensor_tensor_reduce(out=lamj[:, n, :], in0=lamv[:, 2 * n, :], in1=lamv[:, 2 * n + 1, :], scale=1.0,
                                             scalar=0.0, op0=ALU.mult, op1=ALU.add, accum_out=st("LDOT", n, 1))
            ins.then_inc(lam_dot, 1)
            dve.wait_ge(*taken[0])
            v.tensor_scalar(st("NEGMU"), st("SUM"), -1.0 / 512, None, ALU.mult).then_inc(mu_done, 1)
            ahead(g[1])
            dve.wait_ge(vsq_done, 2)
            mean_eps(2, 512, LN_EPS, "VSQ")
            lo_upto(units[g[2]].first + 3)
            inverse(2, 2)
            dve.wait_ge(gain_in, 16 * 3)
            vg = proj[:, :, 2048:2560]
            for t in range(T):
                link(v.scalar_tensor_tensor(out=vg[:, t, :], in0=vg[:, t, :], scalar=st("NEGMU", t, 1),
                                            in1=gain[:, 0:512], op0=ALU.add, op1=ALU.mult))
                v.scalar_tensor_tensor(out=vg[:, t, :], in0=vg[:, t, :], scalar=st("ROOT", t, 1),
                                       in1=gain[:, 512:1024], op0=ALU.mult, op1=ALU.add).then_inc(ln_applied, 1)
            for b in range(2, 4):
                ahead(g[b])
                dve.wait_ge(*taken[block_no[g[b]]])
                tmp = scratch(e, 16, A_HALF)
                x = proj[:, :, 512 * (b - 2):512 * (b - 1)].rearrange("p t (g k) -> p t g k", g=8)[:, :, :, 0:16]
                ins = rope(x, "ropeA", A_HALF, 8, [m[:, :, 8 * (b - 2):8 * (b - 1), :] for m in tmp])
            ins.then_inc(roped, 1)
            for f in range(2):
                k = fills["mixed"] + f
                dve.wait_ge(*filled(k))
                if f == 0:
                    dve.wait_ge(*taken[1])
                for gr in range(4):
                    ub = proj[:, f, 1536 + P * gr:1536 + P * (gr + 1)]
                    ins = v.scalar_tensor_tensor(out=ub, in0=ps[:, 6 + k % 2, P * gr:P * (gr + 1)],
                                                 scalar=sgu_b[:, gr:gr + 1], in1=ub, op0=ALU.add, op1=ALU.mult)
                ins.then_inc(t_free[k % 2], 1)
            evac_half("qk_a", qk_fill(qT, kT, A_QK), 8, 1)
            scores(0, e, A_SCALE, 0)
            ahead(g[4])
            dve.wait_ge(lam_exp, 1)
            link(v.tensor_tensor(st("NLAM"), st("LEXP", 1, 1), st("LEXP", 0, 1), ALU.subtract))
            link(v.tensor_scalar(st("NLAM"), st("NLAM"), LAM_INIT, None, ALU.subtract))
            scores(0, e, A_SCALE, 1)
            oa = proj[:, :, 0:512].rearrange("p t (m d) -> p t m d", m=4)
            for qt in range(T):
                sums(0, qt)
                inv = ("EINV", "EINV1")[qt]
                link(v.tensor_scalar(st(inv, 4, 4), st(inv, 4, 4), st("NLAM"), None, ALU.mult))
                evac_half("pT_a" if qt == 0 else "pT_a1", pT_fill(eT, qt), 2 if qt == 0 else 4, 1)
                dve.wait_ge(o_ready, qt + 1)
                for j in range(2):
                    r = st(inv, 4 * j, 4).rearrange("p (m u) -> p m u", u=1).to_broadcast([P, 4, P])
                    dst = oa[:, qt] if j == 0 else proj[:, qt, 512:1024].rearrange("p (m d) -> p m d", m=4)
                    ins = v.tensor_tensor(dst, ps[:, 4 + j, :].rearrange("p (m d) -> p m d", m=4), r, ALU.mult)
                ins.then_inc(o_free, 1)
                dve.wait_ge(o_free, qt + 1)
                link(v.tensor_tensor(proj[:, qt, 0:512], proj[:, qt, 0:512], proj[:, qt, 512:1024], ALU.add))
            link(v.tensor_tensor(proj[:, :, 512:1024], proj[:, :, 0:512], proj[:, :, 0:512], ALU.mult))
            link(v.reduce_sum(st("SSQ"), proj[:, :, 512:1024].rearrange("p t (m d) -> p t m d", m=4), AX.X))
            mean_eps(8, P)
            inverse(3, 8)
            sb = subln[:, :].rearrange("p (u d) -> p u d", u=1).to_broadcast([P, 4, P])
            for t in range(T):
                r = st("ROOT", 4 * t, 4).rearrange("p (m u) -> p m u", u=1).to_broadcast([P, 4, P])
                link(v.tensor_tensor(oa[:, t], oa[:, t], r, ALU.mult))
                v.scalar_tensor_tensor(out=oa[:, t], in0=oa[:, t], scalar=1.0 - LAM_INIT, in1=sb, op0=ALU.mult,
                                       op1=ALU.mult).then_inc(oa_done, 1)
            rests("cat_even", (xt_hi, xt_lo, KC))

            def residual(u, b):
                ahead(u)
                n = block_no[u]
                dve.wait_ge(*used(u))
                hb = h[:, :, 512 * b:512 * b + 512]
                v.tensor_tensor(hb, hb, ps[:, block_banks(n):block_banks(n) + 2, :], ALU.add).then_inc(h_done, 1)

            for b, u in enumerate(groups["out_even"]):
                residual(u, b)
            dve.wait_ge(h_done, 2)
            rmsnorm(4, 4, halves=True)
            rests("ffn", (xt_hi, xt_lo, KC))
            for f, w in enumerate(widths):
                c = w // P
                ahead(groups["up"][f])
                dve.wait_ge(fsilu, f + 1)
                x = xn[:, 0, :].rearrange("p (c s) -> p c s", c=4)[:, 0:c, :]
                v.tensor_tensor(x, x, ps[:, 0:c, 256:512], ALU.mult).then_inc(fmul, 1)
                dve.wait_ge(f_head, f + 1)
                v.tensor_tensor(f_lo[:, f % 2, 0:c, :], x, f_hi[:, f % 2, 0:c, :].bitcast(F32),
                                ALU.subtract).then_inc(f_done, 1)
            ahead(groups["down"][-1])
            dve.wait_ge(*used(groups["down"][-1]))
            for t in range(T):
                v.tensor_tensor(h[:, t, :], h[:, t, :], flat[:, 2048 + 1024 * t:3072 + 1024 * t],
                                ALU.add).then_inc(down_added, 1)
            dve.wait_ge(down_added, 2)
            rmsnorm(5, 5)
            rests("mix_odd", (xt_hi, xt_lo, KC))
            for u in groups["in_odd"]:
                ahead(u)
            ssq[0] += 4
            dve.wait_ge(ssq_done, ssq[0])
            v.tensor_scalar(st("MS", 0, 2), st("SSQ", 0, 2), 1.0 / CQ, NORM_EPS, ALU.mult, ALU.add)
            v.tensor_scalar(st("MS", 2, 2), st("SSQ", 2, 2), 1.0 / CKV, NORM_EPS, ALU.mult, ALU.add).then_inc(ms_done, 1)
            kpe = proj2[:, :, 1152:1184].rearrange("p t (u k) -> p t u k", u=1)
            link(rope(kpe, "ropeD", D_HALF, 1, [xn[:, :, 768 + 16 * n:784 + 16 * n].rearrange("p t (u k) -> p t u k", u=1)
                                                for n in range(4)]))
            inverse(6, 4)
            dve.wait_ge(gain_in, 16 * 7)
            for n, (a, b, ga) in enumerate(((512, 896, 0), (896, 1152, CQ))):
                for t in range(T):
                    v.scalar_tensor_tensor(out=proj2[:, t, a:b], in0=proj2[:, t, a:b],
                                           scalar=st("ROOT", 2 * n + t, 1), in1=gain[:, ga:ga + b - a],
                                           op0=ALU.mult, op1=ALU.mult).then_inc(xn_done, 1)
            for f in range(4):
                k = fills["poolout"] + f
                heads_seen[0] += 1
                dve.wait_ge(t_head, heads_seen[0])
                v.scalar_tensor_tensor(out=xt_lo[:, f, :], in0=ps[:, 6 + k % 2, 0:256], scalar=pool_s[:, f:f + 1],
                                       in1=xt_hi[:, f, :].bitcast(F32), op0=ALU.mult,
                                       op1=ALU.subtract).then_inc(t_free[k % 2], 1)
            rests("cq", (c_hi, c_lo, 3), count=2)
            rests("ckv", (c_hi, c_lo, 2), count=1, base=3)
            ahead(groups["uq"][0])
            dve.wait_ge(big_free, 1)
            link(rope(qf[:, :, :, D_NOPE:D_QK], "ropeD", D_HALF, MAPS, scratch(e2, MAPS, D_HALF)))
            ahead(groups["ukv"][0])
            v.tensor_copy(kf[:, :, :, D_NOPE:D_QK], kpe.to_broadcast([P, T, MAPS, 2 * D_HALF]))
            dve.wait_ge(big_free, 2)
            v.tensor_copy(kf[:, :, :, 0:D_NOPE], kv[:, :, :, 0:D_NOPE]).then_inc(kf_done, 1)
            evac_half("qk_d", qk_fill(qT2, kT2, D_QK), 8, 1)
            for qt in range(T):
                scores(1, e2, D_SCALE, qt)
            for qt in range(T):
                sums(1, qt)
                evac_half("pT_d" if qt == 0 else "pT_d1", pT_fill(eT2, qt), 2 if qt == 0 else 4, 1)
                dve.wait_ge(o_ready, 3 + qt)
                r = st(("EINV", "EINV1")[qt]).rearrange("p (m u) -> p m u", u=1).to_broadcast([P, MAPS, D_V])
                v.tensor_tensor(proj2[:, qt, 0:512].rearrange("p (m d) -> p m d", m=MAPS),
                                ps[:, 4, :].rearrange("p (m d) -> p m d", m=MAPS), r, ALU.mult).then_inc(o_free, 1)
            rests("cat_odd", (xt_hi, xt_lo, 8), count=2, base=4)
            for b, u in enumerate(groups["out_odd"]):
                residual(u, b)
            dve.wait_ge(h_done, 4)
            rmsnorm(7, 8, halves=True)
            for f in range(4):
                k = fills["router"] + f
                if k % 2 == 1:
                    dve.wait_ge(*filled(k))
                    v.tensor_copy(xT[:, 2 * f:2 * f + 2, :], ps[:, 6 + k % 2, :].rearrange("p (c s) -> p c s", c=2)).then_inc(
                        t_free[k % 2], 1)
            for t in range(T):
                dve.wait_ge(xn_head, t + 1)
                v.tensor_tensor(xn_lo[:, t, :], xn[:, t, :], xn_hi[:, t, :].bitcast(F32), ALU.subtract).then_inc(xn_rest, 1)
            k = fills["logits"]
            dve.wait_ge(*filled(k))
            v.tensor_copy(lg[:, :, :], ps[:, 6 + k % 2, 0:T * NE].rearrange("p (t n) -> p t n", t=T)).then_inc(t_free[k % 2], 1)
            dve.wait_ge(*emptied(k))
            for t in range(T):
                ins = v.max(top[:, t, :], lg[:, t, :])
            link(ins)
            v.tensor_tensor(wts[:, :, 0:1], top[:, :, 1:2], top[:, :, 0:1], ALU.subtract).then_inc(top_done, 1)
            lower = con("lower8").rearrange("p (a b) -> p a b", a=NE)
            for t in range(T):
                mine = lg[:, t, :].rearrange("p (a u) -> p a u", u=1).to_broadcast([P, NE, NE])
                other = lg[:, t, :].rearrange("p (u b) -> p u b", u=1).to_broadcast([P, NE, NE])
                v.tensor_tensor(cmp1[:, t], other, mine, ALU.is_gt)
                link(v.tensor_tensor(cmp2[:, t], other, mine, ALU.is_equal))
                link(v.tensor_tensor(cmp2[:, t], cmp2[:, t], lower, ALU.mult))
                link(v.tensor_tensor(cmp1[:, t], cmp1[:, t], cmp2[:, t], ALU.add))
            link(v.reduce_sum(rank[:, :, :], cmp1[:, :, :, :], AX.X))
            v.tensor_scalar(sel[:, :, :], rank[:, :, :], 2.0, None, ALU.is_lt).then_inc(sel_done, 1)
            v.memset(active[0:1, 0:NE], 1)
            v.memset(active[0:1, ITEMS:ITEMS + 1], 0)
            v.memset(slot_of[:, :, ITEMS:ITEMS + 1], -1.0)
            link(v.memset(expert[0:1, 0:NE], 0))
            k = fills["prefix"]
            dve.wait_ge(*filled(k))
            v.tensor_copy(over[:, 2, :], ps[:, 6 + k % 2, 16:24])
            link(v.tensor_scalar(place[:, :, :], ps[:, 6 + k % 2, 0:T * NE].rearrange("p (t n) -> p t n", t=T), 1.0, None,
                                 ALU.add))
            link(v.tensor_tensor(place[:, :, :], place[:, :, :], sel[:, :, :], ALU.mult))
            link(v.tensor_scalar(slot_of[:, :, 0:NE], place[:, :, :], -1.0, None, ALU.add))

            def gates():
                dve.wait_ge(top_exp, 1)
                link(v.tensor_scalar(wts[:, :, 2:3], wts[:, :, 1:2], 1.0, None, ALU.add))
                link(v.reciprocal(wts[:, :, 2:3], wts[:, :, 2:3]))
                link(v.tensor_tensor(wts[:, :, 3:4], wts[:, :, 1:2], wts[:, :, 2:3], ALU.mult))
                for n in range(2):
                    link(v.tensor_scalar(gtmp[:, :, :], rank[:, :, :], float(n), None, ALU.is_equal))
                    dst = gate if n == 0 else gtmp
                    link(v.tensor_tensor(dst[:, :, :], gtmp[:, :, :], wts[:, :, 2 + n:3 + n].to_broadcast([P, T, NE]), ALU.mult))
                link(v.tensor_tensor(gate[:, :, :], gate[:, :, :], gtmp[:, :, :], ALU.add))
                v.tensor_copy(gate_of[:, :, 0:NE], gate[:, :, :])

            def extras():
                link(v.tensor_scalar(over[:, 0, :], over[:, 2, :], float(SLOTS), None, ALU.is_gt))
                o_row = over[:, 0, :].rearrange("p (u b) -> p u b", u=1)
                link(v.tensor_tensor(cmp1[:, 0], o_row.to_broadcast([P, NE, NE]), lower, ALU.mult))
                link(v.reduce_sum(over[:, 1, :], cmp1[:, 0], AX.X))
                v.tensor_scalar(place[:, :, :], slot_of[:, :, 0:NE], -float(SLOTS), None, ALU.add)
                one = cmp2[:, 0, 0:EXTRA, :]
                nth = con("iota8")[:, 0:EXTRA].rearrange("p (x u) -> p x u", u=1).to_broadcast([P, EXTRA, NE])
                link(v.tensor_tensor(one, over[:, 1, :].rearrange("p (u b) -> p u b", u=1).to_broadcast([P, EXTRA, NE]),
                                     nth, ALU.is_equal))
                link(v.tensor_tensor(one, one, o_row.to_broadcast([P, EXTRA, NE]), ALU.mult))
                v.reduce_sum(over[:, 3, 0:EXTRA], one, AX.X)
                which = con("iota8").rearrange("p (u b) -> p u b", u=1).to_broadcast([P, EXTRA, NE])
                link(v.tensor_tensor(cmp2[:, 1, 0:EXTRA, :], one, which, ALU.mult))
                v.tensor_copy(active[0:1, NE:ITEMS], over[0:1, 3, 0:EXTRA])
                link(v.reduce_sum(over[:, 2, 0:EXTRA], cmp2[:, 1, 0:EXTRA, :], AX.X))
                v.tensor_copy(expert[0:1, NE:ITEMS], over[0:1, 2, 0:EXTRA])
                for src, dst in ((place, slot_of), (gate, gate_of)):
                    for t in range(T):
                        row = src[:, t, :].rearrange("p (u b) -> p u b", u=1).to_broadcast([P, EXTRA, NE])
                        ins = v.tensor_tensor(cmp1[:, t, 0:EXTRA, :], row, one, ALU.mult)
                    link(ins)
                    link(v.reduce_sum(dst[:, :, NE:ITEMS], cmp1[:, :, 0:EXTRA, :], AX.X))
                v.memset(st("JUNK"), 0.0).then_inc(routed, 1)
                dve.wait_ge(routed, 1)

            def expert_rest(i, q):
                j, k = q // 4, q % 4
                dve.wait_ge(hi_done, Q1 + QI * i + q + 1)
                v.tensor_tensor(w_lo[:, (Q1 + q) % NQ, :], slot(j % RING2)[:, 1024 * k:1024 * k + 1024],
                                w_hi[:, (Q1 + q) % NQ, :].bitcast(F32), ALU.subtract).then_inc(lo_done, 1)

            def choose(n):
                for t in range(T):
                    ins = v.tensor_scalar(pick[:, t, :], con("iota"), slot_of[:, t, bass.ds(n, 1)], None, ALU.is_equal)
                ins.then_inc(picked, 1)

            def gathered_rests(n):
                dve.wait_ge(gathered, n + 1)
                v.tensor_copy(xg_lo[:, :, :], ps[:, 2:4, :].rearrange("p b (c s) -> p (b c) s", s=P)).then_inc(xg_rest, 1)

            choose(0)
            for q in range(NQ - 1):
                expert_rest(0, q)
            gates()
            gathered_rests(0)
            expert_rest(0, NQ - 1)
            extras()
            for q in range(NQ, AHEAD):
                expert_rest(0, q)
            v.memset(st("LEFT"), 0.0).then_inc(added, 1)
            with dve.Fori(0, ITEMS) as i:
                on = dve.value_load(active[0:1, bass.ds(i, 1)], min_val=0, max_val=1)
                with dve.If(on > 0):
                    done = [AHEAD]

                    def rests_upto(n):
                        while done[0] < min(n, QI):
                            expert_rest(i, done[0])
                            done[0] += 1

                    def rests_ahead(unit):
                        rests_upto(4 * (pos_of[unit] + 1) + NQ - 1)

                    def hT_rests(f):
                        dve.wait_ge(hT_head, FB * i + f + 1)
                        v.tensor_tensor(hT_lo[:, :, :], ps[:, 7, :].rearrange("p (c s) -> p c s", c=4),
                                        hT_hi[:, :, :].bitcast(F32), ALU.subtract).then_inc(hT_rest, 1)

                    for f in range(FB):
                        if f:
                            rests_ahead(("gate", f))
                            hT_rests(f - 1)
                        rests_ahead(("up", f))
                        dve.wait_ge(silu_done, FB * i + f + 1)
                        if f:
                            dve.wait_ge(hT_ready, FB * i + f)
                        v.tensor_tensor(g_mul, g_act, ps[:, 2 * (f % 2) + 1, :], ALU.mult).then_inc(mul_done, 1)
                        if f == 1:
                            dve.wait_ge(pickT_ready, i + 1)
                            choose(i + 1)
                    rests_ahead(("down", FB - 2))
                    hT_rests(FB - 1)
                    gathered_rests(i + 1)
                    rests_upto(QI)
                    following = dve.value_load(active[0:1, bass.ds(i + 1, 1)], min_val=0, max_val=1)
                    with dve.If(following > 0):
                        for q in range(NQ - 1):
                            expert_rest(i, QI + q)
                    for half in range(2):
                        dve.wait_ge(y_head, 2 * i + half + 1)
                        v.tensor_tensor(y_lo[:, 512 * half:512 * half + 512], ps[:, 4 + half, :],
                                        y_hi[:, 512 * half:512 * half + 512].bitcast(F32),
                                        ALU.subtract).then_inc(y_rest, 1)
                    with dve.If(following > 0):
                        for q in range(NQ - 1, AHEAD):
                            expert_rest(i, QI + q)
                    dve.wait_ge(scattered, i + 1)
                    dve.wait_ge(added, 2 * i + 1)
                    for t in range(T):
                        v.scalar_tensor_tensor(out=h[:, t, :], in0=flat[:, 1024 * (t + 1):1024 * (t + 2)],
                                               scalar=gate_of[:, t, bass.ds(i, 1)], in1=h[:, t, :],
                                               op0=ALU.mult, op1=ALU.add).then_inc(added, 1)
                    dve.wait_ge(added, 2 * i + 3)
                    v.memset(st("MARK"), 0.0)
            v.memset(st("JUNK"), 0.0).then_inc(experts_done, 1)
            ssq[0] += 2
            dve.wait_ge(ssq_done, ssq[0])
            mean_eps(2, D)
            inverse(8, 2)
            dve.wait_ge(gain_in, 16 * 9)
            for t in range(T):
                v.scalar_tensor_tensor(out=xn[:, t, :], in0=h[:, t, :], scalar=st("ROOT", t, 1),
                                       in1=gain[:, :], op0=ALU.mult, op1=ALU.mult).then_inc(out_ready, 1)

        @block.tensor
        def _(pe):
            def bank_free(k):
                if k >= 2:
                    pe.wait_ge(*emptied(k - 2))

            def three(out_, a_hi, a_lo, q, c0, c1, first, last):
                pe.matmul(out_, a_hi, w_hi[:, q, c0:c1], start=first, stop=False)
                pe.matmul(out_, a_hi, w_lo[:, q, c0:c1], start=False, stop=False)
                return pe.matmul(out_, a_lo, w_hi[:, q, c0:c1], start=False, stop=last)

            def transposes(name, src, chunks, norm=None):
                for f in range((chunks + 1) // 2):
                    if norm and f % 2 == 0:
                        pe.wait_ge(*((xn_done, norm_count[norm]) if f else (xn_begun, 2 * norm)))
                    k = fills[name] + f
                    bank_free(k)
                    for c in range(2 * f, min(2 * f + 2, chunks)):
                        for t in range(T):
                            ins = pe.transpose(ps[:, 6 + k % 2, 256 * (c % 2) + P * t:256 * (c % 2) + P * (t + 1)],
                                               src(c, t), ident)
                    ins.then_inc(t_ready[k % 2], 1)

            norm_count = {1: 2, 2: 4, 3: 6, 4: 12}

            def ready_after(name, chunk):
                pe.wait_ge(*emptied(fills[name] + chunk // 2))

            def attention(name, qt_, kt_, w, src_q, src_k, between=None):
                for f in range(8):
                    k = fills["qk_" + name] + f
                    bank_free(k)
                    src = src_q if f < 4 else src_k
                    for mm in range(2):
                        m = 2 * (f % 4) + mm
                        for t in range(T):
                            ins = pe.transpose(ps[0:w, 6 + k % 2, 256 * mm + P * t:256 * mm + P * (t + 1)], src(m, t), ident)
                    ins.then_inc(t_ready[k % 2], 1)
                pe.wait_ge(*emptied(fills["qk_" + name] + 6))
                pe.wait_ge(*emptied(fills["qk_" + name] + 7))
                for m in range(MAPS):
                    ins = pe.matmul(ps[:, 4 + m // 4, P * (m % 4):P * (m % 4 + 1)], qt_[0:w, m, 0:P], kt_[0:w, m, 0:P],
                                    start=True, stop=True)
                ins.then_inc(scored, 1)
                if between:
                    between()
                if name == "a":
                    n = block_no[groups["in_even"][-1]]
                    pe.wait_ge(*taken[n])
                    pe.wait_ge(*taken[n - 1])
                for m in range(MAPS):
                    ins = pe.matmul(ps[:, m // 2, S * (m % 2):S * (m % 2 + 1)], qt_[0:w, m, P:S], kt_[0:w, m, :],
                                    start=True, stop=True)
                ins.then_inc(scored, 1)

            def values(L, name, ee, et, value, dv, qt):
                pe.wait_ge(exped, 2 * L + qt + 1)
                ee = e_first if qt == 0 else ee
                n = 2 if qt == 0 else 4
                base = fills["pT_" + name] + (0 if qt == 0 else 2)
                for f in range(n):
                    k = base + f
                    bank_free(k)
                    kt, m0 = (0, 4 * f) if qt == 0 else (f // 2, 4 * (f % 2))
                    for m in range(4):
                        ins = pe.transpose(ps[:, 6 + k % 2, P * m:P * (m + 1)], ee[:, m0 + m, P * kt:P * (kt + 1)], ident)
                    ins.then_inc(t_ready[k % 2], 1)
                pe.wait_ge(*emptied(base + n - 2))
                pe.wait_ge(*emptied(base + n - 1))
                if qt or L:
                    pe.wait_ge(o_free, 2 * L + qt)
                for m in range(MAPS):
                    o = flat[:, 2048 + dv * m:2048 + dv * (m + 1)]
                    for kt in range(qt + 1):
                        ins = pe.matmul(o, et[:, kt, m, :], value(m, kt), start=(kt == 0), stop=(kt == qt))
                ins.then_inc(o_ready, 1)

            pe.wait_ge(const_in, 16)
            transposes("mix_even", lambda c, t: xn[:, t, P * c:P * (c + 1)], KC, norm=1)

            def run_block(u, name):
                n, unit = block_no[u], units[u]
                if n >= 2:
                    pe.wait_ge(*taken[n - 2])
                w = unit.shape[1]
                for kq in range(unit.quanta):
                    q = unit.first + kq
                    pe.wait_ge(lo_done, q + 1)
                    if name:
                        ready_after(name, 2 * kq)
                    for t in range(T):
                        for c in range(2):
                            kc = 2 * kq + c
                            ins = three(ps[:, block_banks(n) + t, 0:w], xt_hi[:, kc, P * t:P * (t + 1)],
                                        xt_lo[:, kc, P * t:P * (t + 1)], q % NQ, c * w, (c + 1) * w,
                                        kc == 0, kc == KC - 1)
                    ins.then_inc(q_used, 1)

            for b, u in enumerate(groups["in_even"][:4]):
                run_block(u, "mix_even" if b == 0 else None)
            k = fills["sgu_w"]
            bank_free(k)
            pe.wait_ge(sgu_masked, 1)
            for gr in range(4):
                ins = pe.transpose(ps[:, 6 + k % 2, P * gr:P * (gr + 1)], sgu_w[:, gr, :], ident)
            ins.then_inc(t_ready[k % 2], 1)
            pe.wait_ge(*emptied(k))
            for f in range(2):
                k = fills["mixed"] + f
                bank_free(k)
                pe.wait_ge(ln_applied, 2)
                for gr in range(4):
                    ins = pe.matmul(ps[:, 6 + k % 2, P * gr:P * (gr + 1)], sgu_wT[:, gr, :],
                                    proj[:, f, 2048 + P * gr:2048 + P * (gr + 1)], start=True, stop=True)
                ins.then_inc(t_ready[k % 2], 1)
            pe.wait_ge(roped, 1)
            attention("a", qT, kT, A_QK,
                      lambda m, t: proj[:, t, (m % 4) * P + 64 * (m // 4):(m % 4) * P + 64 * (m // 4) + 64],
                      lambda m, t: proj[:, t, 512 + (m % 4) * P + 64 * (m // 4):512 + (m % 4) * P + 64 * (m // 4) + 64],
                      lambda: run_block(groups["in_even"][4], None))
            for qt in range(T):
                values(0, "a", e, eT, lambda m, kt: proj[:, kt, 1024 + P * (m % 4):1024 + P * (m % 4 + 1)], P, qt)
            pe.wait_ge(oa_done, 2)
            transposes("cat_even", lambda c, t: proj[:, t, P * c:P * (c + 1)] if c < 4 else
                       proj[:, t, 1536 + P * (c - 4):1536 + P * (c - 3)], KC)
            for b, u in enumerate(groups["out_even"]):
                run_block(u, "cat_even" if b == 0 else None)
            transposes("ffn", lambda c, t: xn[:, t, P * c:P * (c + 1)], KC, norm=2)

            def ffn_down(f):
                unit = units[groups["down"][f]]
                pe.wait_ge(f_done, f + 1)
                for c in range(unit.quanta):
                    q = unit.first + c
                    pe.wait_ge(lo_done, q + 1)
                    for t in range(T):
                        for half in range(2):
                            ins = three(ps[:, 4 + 2 * t + half, :], f_hi[:, f % 2, c, P * t:P * (t + 1)],
                                        f_lo[:, f % 2, c, P * t:P * (t + 1)], q % NQ, 512 * half, 512 * half + 512,
                                        f == 0 and c == 0, f == len(widths) - 1 and c == unit.quanta - 1)
                    ins.then_inc(q_used, 1)

            for f, w in enumerate(widths):
                nch = w // P
                if f:
                    pe.wait_ge(fmul, f)
                else:
                    pe.wait_ge(h_done, 2)
                for part, name in enumerate(("gate", "up")):
                    unit = units[groups[name][f]]
                    per = KC // unit.quanta
                    for kq in range(unit.quanta):
                        q = unit.first + kq
                        pe.wait_ge(lo_done, q + 1)
                        for c in range(per):
                            kc = kq * per + c
                            if f == 0 and part == 0 and kc % 2 == 0:
                                ready_after("ffn", kc)
                            for fc in range(nch):
                                o = ps[:, fc, 256 * part:256 * part + 256]
                                a, b = c * w + P * fc, c * w + P * (fc + 1)
                                pe.matmul(o, w_hi[:, q % NQ, a:b], xt_hi[:, kc, :], start=(kc == 0), stop=False)
                                pe.matmul(o, w_hi[:, q % NQ, a:b], xt_lo[:, kc, :], start=False, stop=False)
                                ins = pe.matmul(o, w_lo[:, q % NQ, a:b], xt_hi[:, kc, :], start=False, stop=(kc == KC - 1))
                        ins.then_inc(q_used, 1)
                if f:
                    ffn_down(f - 1)
            ffn_down(len(widths) - 1)
            transposes("mix_odd", lambda c, t: xn[:, t, P * c:P * (c + 1)], KC, norm=3)
            for b, u in enumerate(groups["in_odd"]):
                run_block(u, "mix_odd" if b == 0 else None)
            n = block_no[groups["in_odd"][0]]
            pe.wait_ge(*taken[n])
            pe.wait_ge(bands_in, 16)
            for gr in range(4):
                k = fills["pooled"] + gr
                bank_free(k)
                pe.matmul(ps[:, 6 + k % 2, 0:256], proj2[:, 0, P * gr:P * (gr + 1)], bands[:, gr, 0:256], start=True, stop=False)
                ins = pe.matmul(ps[:, 6 + k % 2, P:256], proj2[:, 1, P * gr:P * (gr + 1)], bands[:, gr, 256:384], start=False,
                                stop=True)
                ins.then_inc(t_ready[k % 2], 1)
            pe.wait_ge(odd_in, 32)
            for gr in range(4):
                k = fills["poolout"] + gr
                bank_free(k)
                pe.wait_ge(*emptied(fills["pooled"] + gr))
                pe.matmul(ps[:, 6 + k % 2, 0:256], pool_w[:, gr, :], pooledT[:, gr, :], start=True, stop=True).then_inc(
                    t_ready[k % 2], 1)
            pe.wait_ge(xn_done, 10)
            transposes("cq", lambda c, t: proj2[:, t, 512 + P * c:512 + P * (c + 1)], 3)
            transposes("ckv", lambda c, t: proj2[:, t, 896 + P * c:896 + P * (c + 1)], 2)
            for n, (name, parts, base) in enumerate((("uq", ((0, 512), (512, 768)), 0), ("ukv", ((0, 512), (512, 1024)), 3))):
                unit = units[groups[name][0]]
                if n == 0:
                    b = block_no[groups["in_odd"][2]]
                    pe.wait_ge(*taken[b])
                    pe.wait_ge(*taken[b - 1])
                    pe.wait_ge(*emptied(fills["cq"]))
                    pe.wait_ge(*emptied(fills["cq"] + 1))
                else:
                    pe.wait_ge(big_free, 1)
                    pe.wait_ge(*emptied(fills["ckv"]))
                for c in range(unit.quanta):
                    q = unit.first + c
                    pe.wait_ge(lo_done, q + 1)
                    for t in range(T):
                        for half, (a, b) in enumerate(parts):
                            ins = three(ps[:, 2 * t + half, 0:b - a], c_hi[:, base + c, P * t:P * (t + 1)],
                                        c_lo[:, base + c, P * t:P * (t + 1)], q % NQ, a, b, c == 0, c == unit.quanta - 1)
                    ins.then_inc(q_used, 1)
            pe.wait_ge(kf_done, 1)
            attention("d", qT2, kT2, D_QK, lambda m, t: qf[:, t, m, :], lambda m, t: kf[:, t, m, :])
            for qt in range(T):
                values(1, "d", e2, eT2, lambda m, kt: kv[:, kt, m, D_NOPE:2 * D_NOPE], D_V, qt)
            pe.wait_ge(o_free, 4)
            transposes("cat_odd", lambda c, t: proj2[:, t, P * c:P * (c + 1)], 4)
            pe.wait_ge(*emptied(fills["cat_odd"]))
            pe.wait_ge(*emptied(fills["cat_odd"] + 1))
            for b, u in enumerate(groups["out_odd"]):
                run_block(u, None)
            transposes("router", lambda c, t: xn[:, t, P * c:P * (c + 1)], KC, norm=4)
            k = fills["logits"]
            pe.wait_ge(*emptied(k - 1))
            bank_free(k)
            pe.wait_ge(rw_in, 16)
            for t in range(T):
                for c in range(KC):
                    ins = pe.matmul(ps[:, 6 + k % 2, NE * t:NE * (t + 1)], xT[:, c, P * t:P * (t + 1)], rw[:, c, :],
                                    start=(c == 0), stop=(c == KC - 1))
            ins.then_inc(t_ready[k % 2], 1)
            k = fills["prefix"]
            bank_free(k)
            pe.wait_ge(sel_done, 1)
            before, ones = con("before"), con("ones")
            o = ps[:, 6 + k % 2, :]
            pe.matmul(o[:, 0:NE], before, sel[:, 0, :], start=True, stop=True)
            pe.matmul(o[:, NE:2 * NE], before, sel[:, 1, :], start=True, stop=False)
            pe.matmul(o[:, NE:2 * NE], ones, sel[:, 0, :], start=False, stop=True)
            pe.matmul(o[:, 2 * NE:3 * NE], ones, sel[:, 0, :], start=True, stop=False)
            pe.matmul(o[:, 2 * NE:3 * NE], ones, sel[:, 1, :], start=False, stop=True).then_inc(t_ready[k % 2], 1)
            pe.wait_ge(xn_rest, 2)

            def gather(n):
                pe.wait_ge(picked, n + 1)
                for part, x in enumerate((xn_hi, xn_lo)):
                    for c in range(KC):
                        o = ps[:, 2 * part + c // 4, P * (c % 4):P * (c % 4 + 1)]
                        for t in range(T):
                            ins = pe.matmul(o, x[:, t, P * c:P * (c + 1)], pick[:, t, :], start=(t == 0), stop=(t == T - 1))
                ins.then_inc(gathered, 1)
                for t in range(T):
                    ins = pe.transpose(ps[:, 6, P * t:P * (t + 1)], pick[:, t, :].bitcast(F32), ident)
                ins.then_inc(pickT_ready, 1)

            def gate_up(i, part, quanta_of, first, f):
                for kq in quanta_of:
                    q = 4 * first + kq
                    pe.wait_ge(lo_done, Q1 + QI * i + q + 1)
                    for c in range(2):
                        kc = 2 * kq + c
                        ins = three(ps[:, 2 * (f % 2) + part, :], xg_hi[:, kc, :], xg_lo[:, kc, :], (Q1 + q) % NQ,
                                    512 * c, 512 * c + 512, kc == 0, kc == KC - 1)
                    ins.then_inc(q_used, 1)

            gather(0)
            pe.wait_ge(xg_head, 1)
            pe.wait_ge(xg_rest, 1)
            gate_up(0, 0, range(EARLY), 0, 0)
            pe.wait_ge(routed, 1)
            with pe.Fori(0, ITEMS) as i:
                on = pe.value_load(active[0:1, bass.ds(i, 1)], min_val=0, max_val=1)
                with pe.If(on > 0):
                    def hidden(f):
                        pe.wait_ge(mul_done, FB * i + f + 1)
                        if f:
                            pe.wait_ge(hT_rest, FB * i + f)
                        for c in range(4):
                            ins = pe.transpose(ps[:, 7, P * c:P * (c + 1)], g_mul[:, P * c:P * (c + 1)], ident)
                        ins.then_inc(hT_ready, 1)

                    def down(f):
                        pe.wait_ge(hT_rest, FB * i + f + 1)
                        for c in range(4):
                            q = 4 * pos_of[("down", f)] + c
                            pe.wait_ge(lo_done, Q1 + QI * i + q + 1)
                            for half in range(2):
                                ins = three(ps[:, 4 + half, :], hT_hi[:, c, :], hT_lo[:, c, :], (Q1 + q) % NQ,
                                            512 * half, 512 * half + 512, f == 0 and c == 0, f == FB - 1 and c == 3)
                            ins.then_inc(q_used, 1)

                    for f in range(FB):
                        if f == 1:
                            pe.wait_ge(added, 2 * i + 1)
                        if f >= 2:
                            pe.wait_ge(mul_done, FB * i + f - 1)
                        gate_up(i, 0, range(0 if f else EARLY, 4), pos_of[("gate", f)], f)
                        if f:
                            hidden(f - 1)
                        gate_up(i, 1, range(4), pos_of[("up", f)], f)
                        if f:
                            down(f - 1)
                    hidden(FB - 1)
                    pe.wait_ge(pickT_done, i + 1)
                    gather(i + 1)
                    down(FB - 1)
                    pe.wait_ge(xg_head, i + 2)
                    pe.wait_ge(xg_rest, i + 2)
                    following = pe.value_load(active[0:1, bass.ds(i + 1, 1)], min_val=0, max_val=1)
                    with pe.If(following > 0):
                        gate_up(i, 0, range(EARLY), UI, 0)
                    for half in range(2):
                        pe.wait_ge(y_rest, 2 * i + half + 1)
                        for t in range(T):
                            o = ps[:, 2 * (t + 1) + half, :]
                            pe.matmul(o, pickT[:, P * t:P * (t + 1)], y_hi[:, 512 * half:512 * half + 512], start=True, stop=False)
                            ins = pe.matmul(o, pickT[:, P * t:P * (t + 1)], y_lo[:, 512 * half:512 * half + 512], start=False,
                                            stop=True)
                    ins.then_inc(scattered, 1)


INS = ["x", "norm_mix_even", "w_in_even", "lam_q1", "lam_k1", "lam_q2", "lam_k2", "subln_g", "sgu_ln_g", "sgu_ln_b",
       "sgu_w", "sgu_b", "w_out_even", "norm_ffn_even", "ffn_wg", "ffn_wu", "ffn_wd", "norm_mix_odd", "w_in_odd",
       "pool_w", "pool_scale", "q_norm_g", "w_uq", "kv_norm_g", "w_ukv", "w_out_odd", "norm_ffn_odd", "router",
       "moe_wg", "moe_wu", "moe_wd", "final_norm"]


def kernel(**inputs):
    import numpy as np
    import concourse.bacc as bacc
    from concourse.bass_utils import run_bass_kernel_spmd as run

    nc = bacc.Bacc("TRN2", target_bir_lowering=False, num_devices=1)
    arrays = {f"in_{n}": np.ascontiguousarray(inputs[n]) for n in INS}
    arrays["consts"], arrays["bands"] = constants()
    aps = {n: nc.dram_tensor(n, a.shape, mybir.dt.from_np(a.dtype), kind="ExternalInput").ap()
           for n, a in arrays.items()}
    out = nc.dram_tensor("out_0", (1, S, D), F32, kind="ExternalOutput").ap()
    trunk(nc, {n: aps[f"in_{n}"] for n in INS}, aps["consts"], aps["bands"], out)
    r = run(nc, [arrays], core_ids=[0])
    return r.results[0]["out_0"]
```
